# Optimizing a Trainium2 kernel written in Bass

```python
import jax, jax.numpy as jnp
from jax import lax
import numpy as np

D_MODEL = 1024
BATCH = 1
SEQ = 256
DEPTH = 1

HEAD_DIM = 64
ATTN_WIDTH = D_MODEL // 2
POOL_WIDTH = D_MODEL - ATTN_WIDTH
MIX_WIDTH = ATTN_WIDTH + POOL_WIDTH
N_Q_HEADS = ATTN_WIDTH // HEAD_DIM
GQA_GROUP = 4
N_KV_HEADS = N_Q_HEADS // GQA_GROUP
KV_WIDTH = N_KV_HEADS * HEAD_DIM
IN_PROJ_WIDTH = ATTN_WIDTH + 2 * KV_WIDTH + POOL_WIDTH
WINDOW = 128
ATTN_BLOCK = 128
ROPE_THETA = 500000.0
ROPE_DIM = HEAD_DIM // 4
POOL_WINDOWS = (2, 4, 8, 16)
N_POOL_GROUPS = len(POOL_WINDOWS)
POOL_GROUP_WIDTH = POOL_WIDTH // N_POOL_GROUPS
N_EXPERTS = 32
TOP_K = 4
D_FF = D_MODEL
SWIGLU_LIMIT = 7.0
SWIGLU_ALPHA = 1.702
EXPERT_BLOCK = 256
NORM_EPS = 1e-5
QK_NORM_EPS = 1e-6
NEG_INF = -1e30

kernel_name = 'hymba_swa_sink_pool_moe_layer'

def rms_norm(x, w, eps):
    xf = x.astype(jnp.float32)
    y = xf * lax.rsqrt(jnp.mean(xf * xf, axis=-1, keepdims=True) + eps)
    return (y * w.astype(jnp.float32)).astype(x.dtype)

def partial_rope(x, cos, sin):
    half = ROPE_DIM // 2
    r = x[..., :ROPE_DIM].astype(jnp.float32)
    x1, x2 = r[..., :half], r[..., half:]
    rot = jnp.concatenate([x1 * cos - x2 * sin, x2 * cos + x1 * sin], axis=-1).astype(x.dtype)
    return jnp.concatenate([rot, x[..., ROPE_DIM:]], axis=-1)

def sliding_window_attention(q, k, v, sinks):
    B, S, Hkv, G, D = q.shape
    n_blocks = S // ATTN_BLOCK
    pad = ((0, 0), (ATTN_BLOCK, 0), (0, 0), (0, 0))
    kp = jnp.pad(k, pad)
    vp = jnp.pad(v, pad)
    qi = jnp.arange(ATTN_BLOCK)[:, None]
    kj = jnp.arange(2 * ATTN_BLOCK)[None, :]
    band = (kj <= qi + ATTN_BLOCK) & (kj > qi + ATTN_BLOCK - WINDOW)
    sink = sinks.astype(jnp.float32).reshape(1, Hkv, G, 1, 1)
    scale = HEAD_DIM ** -0.5

    def one_block(i):
        start = i * ATTN_BLOCK
        qb = lax.dynamic_slice_in_dim(q, start, ATTN_BLOCK, axis=1)
        kb = lax.dynamic_slice_in_dim(kp, start, 2 * ATTN_BLOCK, axis=1)
        vb = lax.dynamic_slice_in_dim(vp, start, 2 * ATTN_BLOCK, axis=1)
        s = jnp.einsum('bqhgd,bkhd->bhgqk', qb, kb).astype(jnp.float32) * scale
        valid = band & (start - ATTN_BLOCK + kj >= 0)
        s = jnp.where(valid, s, NEG_INF)
        sink_col = jnp.broadcast_to(sink, s.shape[:-1] + (1,))
        probs = jax.nn.softmax(jnp.concatenate([s, sink_col], axis=-1), axis=-1)[..., :-1]
        return jnp.einsum('bhgqk,bkhd->bqhgd', probs.astype(vb.dtype), vb)

    out = lax.map(one_block, jnp.arange(n_blocks))
    out = jnp.moveaxis(out, 0, 1)
    return out.reshape(B, S, Hkv * G * D)

def multiscale_pool(u, pool_w, pool_scale):
    B, S, _ = u.shape
    uf = u.astype(jnp.float32).reshape(B, S, N_POOL_GROUPS, POOL_GROUP_WIDTH)
    csum = jnp.cumsum(uf, axis=1)
    pos1 = jnp.arange(S) + 1
    groups = []
    for g, w in enumerate(POOL_WINDOWS):
        c = csum[:, :, g]
        lagged = jnp.pad(c[:, :S - w], ((0, 0), (w, 0), (0, 0)))
        count = jnp.minimum(pos1, w).astype(jnp.float32)[None, :, None]
        groups.append((c - lagged) / count - uf[:, :, g])
    pooled = jnp.stack(groups, axis=2)
    mixed = jnp.einsum('bsgc,gcd->bsgd', pooled, pool_w.astype(jnp.float32))
    return (mixed.reshape(B, S, POOL_WIDTH) * pool_scale.astype(jnp.float32)).astype(u.dtype)

def moe_ffn(h, w_router, b_router, w_gu, b_gu, w_down, b_down):
    T = h.shape[0]
    n_assign = T * TOP_K
    logits = (h @ w_router).astype(jnp.float32) + b_router.astype(jnp.float32)
    top_v, top_i = lax.top_k(logits, TOP_K)
    gates = jax.nn.softmax(top_v, axis=-1)
    e_flat = top_i.reshape(-1)
    g_flat = gates.reshape(-1)
    tok_flat = jnp.arange(n_assign, dtype=jnp.int32) // TOP_K
    order = jnp.argsort(e_flat)
    e_sorted = e_flat[order]
    counts = jnp.bincount(e_flat, length=N_EXPERTS)
    start = jnp.cumsum(counts) - counts
    padded = ((counts + EXPERT_BLOCK - 1) // EXPERT_BLOCK) * EXPERT_BLOCK
    pend = jnp.cumsum(padded)
    pstart = pend - padded
    slot = pstart[e_sorted] + (jnp.arange(n_assign) - start[e_sorted])
    n_slots = -(-n_assign // EXPERT_BLOCK) * EXPERT_BLOCK + N_EXPERTS * EXPERT_BLOCK
    n_blk = n_slots // EXPERT_BLOCK
    slot_tok = jnp.zeros((n_slots,), jnp.int32).at[slot].set(tok_flat[order])
    slot_gate = jnp.zeros((n_slots,), jnp.float32).at[slot].set(g_flat[order])
    blk_start = jnp.arange(n_blk, dtype=pend.dtype) * EXPERT_BLOCK
    blk_expert = jnp.minimum(jnp.searchsorted(pend, blk_start, side='right'), N_EXPERTS - 1)

    def expert_block(args):
        e, toks, gw = args
        xb = h[toks]
        gu = xb @ w_gu[e] + b_gu[e]
        gate = jnp.minimum(gu[:, :D_FF], SWIGLU_LIMIT)
        up = jnp.clip(gu[:, D_FF:], -SWIGLU_LIMIT, SWIGLU_LIMIT)
        act = gate * jax.nn.sigmoid(gate * SWIGLU_ALPHA) * (up + 1.0)
        y = act @ w_down[e] + b_down[e]
        return (y * gw[:, None]).astype(h.dtype)

    y = lax.map(expert_block, (blk_expert,
                               slot_tok.reshape(n_blk, EXPERT_BLOCK),
                               slot_gate.reshape(n_blk, EXPERT_BLOCK)))
    return jax.ops.segment_sum(y.reshape(n_slots, -1), slot_tok, num_segments=T)

def setup_inputs(seed: int = 0) -> dict:
    key = jax.random.key(seed)
    ks = jax.random.split(key, 18)
    f32 = jnp.float32
    nrm = lambda k, shape, s: jax.random.normal(k, shape, f32) * s
    x = jax.random.normal(ks[0], (BATCH, SEQ, D_MODEL), f32)
    offsets = jax.random.randint(ks[1], (BATCH, 1), 0, SEQ, dtype=jnp.int32)
    positions = offsets + jnp.arange(SEQ, dtype=jnp.int32)[None, :]
    return {
        'x': x,
        'positions': positions,
        'norm1_w': 1.0 + nrm(ks[2], (D_MODEL,), 0.02),
        'w_in': nrm(ks[3], (D_MODEL, IN_PROJ_WIDTH), D_MODEL ** -0.5),
        'q_norm_w': 1.0 + nrm(ks[4], (HEAD_DIM,), 0.02),
        'k_norm_w': 1.0 + nrm(ks[5], (HEAD_DIM,), 0.02),
        'sinks': nrm(ks[6], (N_Q_HEADS,), 0.5),
        'pool_w': nrm(ks[7], (N_POOL_GROUPS, POOL_GROUP_WIDTH, POOL_GROUP_WIDTH), POOL_GROUP_WIDTH ** -0.5),
        'pool_scale': 1.0 + nrm(ks[8], (POOL_WIDTH,), 0.1),
        'w_out': nrm(ks[9], (MIX_WIDTH, D_MODEL), MIX_WIDTH ** -0.5),
        'norm2_w': 1.0 + nrm(ks[10], (D_MODEL,), 0.02),
        'w_router': nrm(ks[11], (D_MODEL, N_EXPERTS), D_MODEL ** -0.5),
        'b_router': nrm(ks[12], (N_EXPERTS,), 0.01),
        'w_gu': nrm(ks[13], (N_EXPERTS, D_MODEL, 2 * D_FF), D_MODEL ** -0.5),
        'b_gu': nrm(ks[14], (N_EXPERTS, 2 * D_FF), 0.02),
        'w_down': nrm(ks[15], (N_EXPERTS, D_FF, D_MODEL), D_FF ** -0.5),
        'b_down': nrm(ks[16], (N_EXPERTS, D_MODEL), 0.02),
    }

def reference(x, positions, norm1_w, w_in, q_norm_w, k_norm_w, sinks, pool_w, pool_scale,
              w_out, norm2_w, w_router, b_router, w_gu, b_gu, w_down, b_down):
    B, S, _ = x.shape
    inv_freq = ROPE_THETA ** (-jnp.arange(0, ROPE_DIM, 2, dtype=jnp.float32) / ROPE_DIM)
    ang = positions.astype(jnp.float32)[..., None] * inv_freq
    cos = jnp.cos(ang)[:, :, None, :]
    sin = jnp.sin(ang)[:, :, None, :]

    h = x
    for _ in range(DEPTH):
        n = rms_norm(h, norm1_w, NORM_EPS)
        proj = n @ w_in
        q = proj[..., :ATTN_WIDTH].reshape(B, S, N_Q_HEADS, HEAD_DIM)
        k = proj[..., ATTN_WIDTH:ATTN_WIDTH + KV_WIDTH].reshape(B, S, N_KV_HEADS, HEAD_DIM)
        v = proj[..., ATTN_WIDTH + KV_WIDTH:ATTN_WIDTH + 2 * KV_WIDTH].reshape(B, S, N_KV_HEADS, HEAD_DIM)
        u = proj[..., ATTN_WIDTH + 2 * KV_WIDTH:]
        q = partial_rope(rms_norm(q, q_norm_w, QK_NORM_EPS), cos, sin)
        k = partial_rope(rms_norm(k, k_norm_w, QK_NORM_EPS), cos, sin)
        q = q.reshape(B, S, N_KV_HEADS, GQA_GROUP, HEAD_DIM)
        attn_out = sliding_window_attention(q, k, v, sinks)
        pool_out = multiscale_pool(u, pool_w, pool_scale)
        mixed = jnp.concatenate([attn_out, pool_out.astype(attn_out.dtype)], axis=-1)
        h = h + mixed @ w_out
        n2 = rms_norm(h, norm2_w, NORM_EPS).reshape(B * S, D_MODEL)
        h = h + moe_ffn(n2, w_router, b_router, w_gu, b_gu, w_down, b_down).reshape(B, S, D_MODEL)
    return h


_drawn_inputs = setup_inputs


def setup_inputs(seed=0):
    import zlib

    import numpy as np

    out = dict(_drawn_inputs(seed))
    spreads = {}
    factors = {'q_norm_w': 3.876,
     'k_norm_w': 4.154,
     'sinks': 13.515,
     'b_gu': 5.899,
     'b_down': 6.769,
     'b_router': 2.685}
    for name, (base, spread) in spreads.items():
        noise = np.random.default_rng([zlib.crc32(name.encode()), seed]).standard_normal(out[name].shape)
        drawn = base * np.exp(spread * noise) if base else spread * noise
        out[name] = __import__('jax').numpy.asarray(drawn.astype(out[name].dtype))
    for name, factor in factors.items():
        out[name] = (out[name] * factor).astype(out[name].dtype)
    return out
```

```python
from contextlib import ExitStack

import numpy as np
import concourse.bass as bass
from concourse import mybir

F32 = mybir.dt.float32
I32 = mybir.dt.int32
U32 = mybir.dt.uint32
ALU = mybir.AluOpType
ACT = mybir.ActivationFunctionType
AX_X = mybir.AxisListType.X

P = 128
SEQ, DM = 256, 1024
T = SEQ // P
KC = DM // P
HD = 64
NQ, NKV = 8, 2
NH = NQ + NKV
GRP = NQ // NKV
QKW = NH * HD
ATT = NQ * HD
VW = NKV * HD
PW = DM - ATT
INW = QKW + VW + PW
WINDOW = 128
HALF = HD // 4 // 2
POOLS = (2, 4, 8, 16)
NG = len(POOLS)
NE, TOPK, FF = 32, 4, 1024
LIMIT, ALPHA = 7.0, 1.702
EPS, QK_EPS = 1e-5, 1e-6
NEG = -1e30
SLOTS = 64
PASSES = SEQ // SLOTS
PIECES = 6
GU_PIECES = 4
PIECE = 4096
ROUNDS = 3
NR = NE * PASSES + NE

C_ID, C_TRI, C_ONE, C_MASK, C_IOTA, C_FREQ = 0, 128, 256, 384, 640, 768
NC_COLS = 776

TWO_PI_INV = float(np.float32(1.0 / (2.0 * np.pi)))
PI_A = 6.28125
PI_B = float(np.float32(np.float32((2.0 * np.pi - PI_A) * 2.0**21).round() / 2.0**21))
PI_C = float(np.float32(2.0 * np.pi - PI_A - PI_B))
ROUND = 12582912.0
SIN_MAX = 3.1415925
RSQRT_MAGIC = 1597463007.0


def shape_constants():
    c = np.zeros((P, NC_COLS), np.float32)
    i = np.arange(P)
    c[:, C_ID:C_ID + P] = np.eye(P)
    c[:, C_TRI:C_TRI + P] = i[:, None] < i[None, :]
    c[:, C_ONE:C_ONE + P] = 1.0
    c[:, C_MASK:C_MASK + P] = np.where(i[None, :] > i[:, None] + P - WINDOW, 0.0, NEG)
    c[:, C_MASK + P:C_MASK + 2 * P] = np.where(i[None, :] <= i[:, None], 0.0, NEG)
    c[:, C_IOTA:C_IOTA + P] = np.tile(np.arange(SLOTS), P // SLOTS)[None, :]
    c[:, C_FREQ:C_FREQ + HALF] = np.float32(500000.0) ** (-np.arange(0, 2 * HALF, 2, dtype=np.float32) / (2 * HALF))
    bands = np.zeros((P, NG, SEQ + P), np.float32)
    s = np.arange(SEQ)
    for g, w in enumerate(POOLS):
        full = ((s[:, None] <= s[None, :]) & (s[:, None] > s[None, :] - w)) / np.minimum(s + 1, w)[None, :] - np.eye(SEQ)
        bands[:, g, :SEQ] = full[:P]
        bands[:, g, SEQ:] = full[P:, P:]
    return c, bands.reshape(P, NG * (SEQ + P))


def layer_kernel(nc, x, positions, norm1_w, w_in, q_norm_w, k_norm_w, sinks, pool_w, pool_scale,
                 w_out, norm2_w, w_router, b_router, w_gu, b_gu, w_down, b_down, consts, bands, out):
    x_t = x.rearrange("b (t p) d -> p (b t) d", p=P)
    out_t = out.rearrange("b (t p) d -> (b t) p d", p=P)
    w_in_k = w_in.rearrange("(k p) n -> p k n", p=P)
    w_out_a = w_out[0:ATT, :].rearrange("(g h d) n -> g d h n", g=NKV, d=HD)
    w_out_p = w_out[ATT:DM, :].rearrange("(k p) n -> p k n", p=P)
    w_gu_k = w_gu.rearrange("e (k p) n -> p (e k) n", p=P)
    w_dn_k = w_down.rearrange("e (k p) n -> p (e k) n", p=P)

    with ExitStack() as ctx:
        def sb(name, shape, dt=F32):
            return ctx.enter_context(nc.sbuf_tensor(name, shape, dt))

        def sem(name):
            return ctx.enter_context(nc.semaphore(name))

        ring = sb("ring", [P, PIECES * PIECE])
        X = sb("X", [P, T, DM])
        N2 = sb("N2", [P, T, DM])
        bgu = sb("bgu", [P, 2 * FF])
        shared = sb("shared", [P, 8 * DM])
        tT = sb("tT", [P, KC, SEQ])
        qk = sb("qk", [P, T, QKW])
        U = sb("U", [P, T, PW])
        V = sb("V", [P, T, VW])
        qT = sb("qT", [P, GRP, SEQ])
        kT = sb("kT", [P, SEQ])
        PR = sb("PR", [P, 2, 1024])
        PT = sb("PT", [P, 2, 1024])
        mixA = sb("mixA", [P, GRP, SEQ])
        mixP = sb("mixP", [P, NG, SEQ])
        C = sb("C", [P, NC_COLS])
        wr = sb("wr", [P, KC, NE])
        small = sb("small", [P, 520])

        front = ring[:, 3 * PIECE:6 * PIECE]
        win = front[:, 0:KC * INW].rearrange("p (k n) -> p k n", k=KC)
        band = front[:, KC * INW:KC * INW + NG * (SEQ + P)].rearrange("p (g s) -> p g s", g=NG)
        poolw = front[:, KC * INW + NG * (SEQ + P):3 * PIECE].rearrange("p (g n) -> p g n", g=NG)
        wout = shared[:, :].rearrange("p (k n) -> p k n", k=KC)
        pooled = PT[:, 1, :].rearrange("p (g s) -> p g s", g=NG)
        w2b = U[:, :, :].rearrange("p t n -> p (t n)")
        bdn = mixP[:, :, :].rearrange("p g s -> p (g s)")[0:NE, :]
        tmp = PR[:, 1, :]

        ident = C[:, C_ID:C_ID + P]
        tri = C[:, C_TRI:C_TRI + P]
        ones = C[:, C_ONE:C_ONE + P]
        iota = C[:, C_IOTA:C_IOTA + P]

        at = [0]

        def cut(n, of=small):
            at[0] += n
            return of[:, at[0] - n:at[0]]

        w1c = cut(KC)
        scl = cut(NG)
        qnw, knw = cut(HD), cut(HD)
        sink = cut(NQ)
        brt = cut(NE)
        posi, posf = cut(T), cut(T)
        trig = cut(T * 2 * HALF).rearrange("p (t f h) -> p t f h", t=T, f=2)
        turn = cut(T * 2 * HALF).rearrange("p (t f h) -> p t f h", t=T, f=2)
        ss, rs, rt = cut(NH), cut(NH), cut(NH)
        nrm = cut(2)
        mx, nm, es, sm, rc = cut(8), cut(8), cut(8), cut(8), cut(8)
        lg, lm = cut(T * NE).rearrange("p (t e) -> p t e", t=T), cut(T)
        top, idf, gts, gsum = (cut(T * 8).rearrange("p (t e) -> p t e", t=T) for _ in range(4))
        assert at[0] <= 520

        at[0] = 0
        xe = cut(KC * SLOTS, shared).rearrange("p (k s) -> p k s", k=KC)
        gb, sg, ub, ab = (cut(512, shared).rearrange("p (b n) -> p b n", b=2) for _ in range(4))
        aT = cut(512, shared).rearrange("p (f s) -> p f s", f=4)
        ye = cut(512, shared)
        GT = cut(2 * P, shared).rearrange("p (t s) -> p t s", t=T)
        S1 = cut(T * SLOTS, shared).rearrange("p (t s) -> p t s", t=T)
        SG = cut(T * P, shared).rearrange("p (t s) -> p t s", t=T)
        oneh = cut(SLOTS, shared)
        rank = cut(T * NR, shared).rearrange("p (t e) -> p t e", t=T)
        gate = cut(T * NR, shared).rearrange("p (t e) -> p t e", t=T)
        sel = cut(T * NE, shared).rearrange("p (t e) -> p t e", t=T)
        Gd = cut(T * NE, shared).rearrange("p (t e) -> p t e", t=T)
        GdT = cut(T * P, shared).rearrange("p (t s) -> p t s", t=T)[0:NE]
        cnt = cut(1, shared)
        cnti = cut(1, shared)
        topi = cut(T * 8, shared).rearrange("p (t e) -> p t e", t=T)
        rk = cut(T * NE, shared).rearrange("p (t e) -> p t e", t=T)
        assert at[0] <= 8 * DM

        ps = ctx.enter_context(nc.psum_tensor("ps", [P, 8, 512], F32))
        Q_BANK, U_BANK, KV_BANK = (0, 3), (2, 4), (1, 5)
        SET = ((0, 1), (6, 7), (0, 1))
        ACC = (2, 4)
        GU, GAT, DWN = 6, 0, 1

        ld_x = [sem(f"ld_x{t}") for t in range(T)]
        ld_c, ld_small, ld_bands = sem("ld_c"), sem("ld_small"), sem("ld_bands")
        ld_win = [sem(f"ld_win{k}") for k in range(KC)]
        ld_wout, ld_w2, ld_bdn, ld_bgu = sem("ld_wout"), sem("ld_w2"), sem("ld_bdn"), sem("ld_bgu")
        landed = [sem(f"landed{c}") for c in range(PIECES)]
        zeroed = sem("zeroed")
        stored = sem("stored")
        dv = sem("dv")
        x_ss = sem("x_ss")
        xT_psum, xT_sb, proj = sem("xT_psum"), sem("xT_sb"), sem("proj")
        rstd1 = sem("rstd1")
        trig_arg, trig_done = sem("trig_arg"), sem("trig_done")
        qk_out, uv_out, roped = sem("qk_out"), sem("uv_out"), sem("roped")
        qkT_psum, qkT_sb = sem("qkT_psum"), sem("qkT_sb")
        scores, maxed, exped, probs = sem("scores"), sem("maxed"), sem("exped"), sem("probs")
        PT_psum, PT_a, PT_v = sem("PT_psum"), sem("PT_a"), sem("PT_v")
        oT_psum, oT_sb = sem("oT_psum"), sem("oT_sb")
        pooled_psum, pooled_sb, mix_psum, mix_sb = sem("pooled_psum"), sem("pooled_sb"), sem("mix_psum"), sem("mix_sb")
        pool_used = sem("pool_used")
        h_psum, h_sb, h_ss, n2_sb = sem("h_psum"), sem("h_sb"), sem("h_ss"), sem("n2_sb")
        n2T_psum, n2T_a, n2T_v, logits = sem("n2T_psum"), sem("n2T_a"), sem("n2T_v"), sem("logits")
        top_in, top_exp, gates = sem("top_in"), sem("top_exp"), sem("gates")
        ranks, GdT_psum, GdT_sb, count_ready = sem("ranks"), sem("GdT_psum"), sem("GdT_sb"), sem("count_ready")
        pieces_used = sem("pieces_used")
        s_ready, sg_ready, oneh_ready = sem("s_ready"), sem("sg_ready"), sem("oneh_ready")
        gathered, xe_sb = sem("gathered"), sem("xe_sb")
        gu_done, gu_free, g_ready, sig_ready, act_ready = sem("gu_done"), sem("gu_free"), sem("g_ready"), sem("sig_ready"), sem("act_ready")
        u_ready, ug_ready = sem("u_ready"), sem("ug_ready")
        aT_psum, aT_sb = sem("aT_psum"), sem("aT_sb")
        gt_psum, gt_sb, y_sb = sem("gt_psum"), sem("gt_sb"), sem("y_sb")
        acc_final, out_sb = sem("acc_final"), sem("out_sb")

        block = ctx.enter_context(nc.Block())

        def more_passes(eng, body):
            eng.wait_ge(count_ready, 1)
            most = eng.value_load(cnti[0:1, 0:1].bitcast(I32), min_val=0, max_val=SEQ)
            with eng.If(most > SLOTS):
                with eng.Fori(1, PASSES) as p:
                    with eng.Fori(0, NE) as e:
                        body(p, e)

        @block.sync
        def _(sp):
            for t in range(T):
                sp.dma_start(X[:, t, :], x_t[:, t, :]).then_inc(ld_x[t], 16)
            for k in range(KC):
                sp.dma_start(win[:, k, :], w_in_k[:, k, :]).then_inc(ld_win[k], 16)
            sp.dma_start(band, bands.rearrange("p (g s) -> p g s", g=NG)).then_inc(ld_bands, 16)
            sp.dma_start(poolw, pool_w.rearrange("g c d -> c g d")).then_inc(ld_bands, 16)
            sp.dma_start(wout[:, GRP:KC, :], w_out_p).then_inc(ld_wout, 16)
            for g in range(NKV):
                sp.dma_start(wout[g * HD:(g + 1) * HD, 0:GRP, :], w_out_a[g]).then_inc(ld_wout, 16)

            def load_piece(c, e):
                if c < GU_PIECES:
                    dst = ring[:, c * PIECE:(c + 1) * PIECE].rearrange("p (k n) -> p k n", k=2)
                    src = w_gu_k[:, bass.ds(e * KC + 2 * c, 2), :]
                else:
                    dst = ring[:, c * PIECE:(c + 1) * PIECE].rearrange("p (k n) -> p k n", k=4)
                    src = w_dn_k[:, bass.ds(e * KC + 4 * (c - GU_PIECES), 4), :]
                sp.dma_start(dst, src).then_inc(landed[c], 16)

            for c in range(3):
                load_piece(c, 0)
            sp.wait_ge(proj, 3)
            for c in range(3, 5):
                load_piece(c, 0)
            sp.wait_ge(mix_psum, 1)
            load_piece(5, 0)
            sp.wait_ge(pooled_psum, 1)
            sp.dma_start(w2b, norm2_w.rearrange("(a n) -> a n", a=1).to_broadcast([P, DM])).then_inc(ld_w2, 16)
            sp.wait_ge(pool_used, 1)
            sp.dma_start(bdn, b_down).then_inc(ld_bdn, 16)

            with sp.Fori(0, NE - 1) as e:
                for c in range(PIECES):
                    sp.wait_ge(pieces_used, e * PIECES + c + 1)
                    load_piece(c, e + 1)

            def next_pass(p, e):
                for c in range(PIECES):
                    sp.wait_ge(pieces_used, p * (NE * PIECES) + e * PIECES + (c + 1 - PIECES))
                    load_piece(c, e)

            more_passes(sp, next_pass)

            for t in range(T):
                sp.wait_ge(out_sb, t + 1)
                sp.dma_start(out_t[t], X[:, t, :]).then_inc(stored, 16)
            sp.wait_ge(stored, 16 * T)

        @block.gpsimd
        def _(pool):
            nc.gpsimd.memset(bgu[:, :], 0.0).then_inc(zeroed, 1)

        @block.scalar
        def _(act):
            act.dma_start(C[:, :], consts).then_inc(ld_c, 16)
            act.dma_start(w1c, norm1_w.rearrange("(k p) -> p k", p=P), allow_slow_non_contiguous=True).then_inc(ld_c, 16)
            act.dma_start(posi.bitcast(I32), positions.rearrange("b (t p) -> p (b t)", p=P), allow_slow_non_contiguous=True).then_inc(ld_small, 16)
            act.dma_start(scl, pool_scale.rearrange("(g p) -> p g", p=P), allow_slow_non_contiguous=True).then_inc(ld_small, 16)
            for dst, src in ((qnw, q_norm_w), (knw, k_norm_w), (sink, sinks), (brt, b_router)):
                row = src.rearrange("(a n) -> a n", a=1)
                act.dma_start(dst, row.to_broadcast([P, row.shape[1]])).then_inc(ld_small, 16)
            act.dma_start(wr[:, :, :], w_router.rearrange("(k p) e -> p k e", p=P)).then_inc(ld_small, 16)
            act.wait_ge(zeroed, 1)
            act.dma_start(bgu[0:NE, :], b_gu).then_inc(ld_bgu, 16)

            for t in range(T):
                act.wait_ge(ld_x[t], 16)
                nc.scalar.activation(PR[:, t, :], X[:, t, :], ACT.Square, accum_out=nrm[:, t:t + 1]).then_inc(x_ss, 1)
            act.wait_ge(trig_arg, 1)
            nc.scalar.activation(trig, turn, ACT.Sin).then_inc(trig_done, 1)

            def proj_out(t, src, dst, s):
                nc.scalar.activation(dst, src, ACT.Copy, scale=rc[:, t:t + 1]).then_inc(s, 1)

            def qkv_out(t):
                act.wait_ge(proj, t + 1)
                for g in range(NKV):
                    proj_out(t, ps[:, Q_BANK[t], g * GRP * HD:(g + 1) * GRP * HD].rearrange("p (h d) -> p h d", h=GRP),
                             qk[:, t, 0:ATT].rearrange("p (h g d) -> p g h d", g=NKV, h=GRP)[:, g], qk_out)
                proj_out(t, ps[:, KV_BANK[t], 0:VW], qk[:, t, ATT:QKW], qk_out)
                proj_out(t, ps[:, KV_BANK[t], VW:2 * VW], V[:, t, :], uv_out)

            act.wait_ge(rstd1, 1)
            qkv_out(0)
            proj_out(0, ps[:, U_BANK[0], :], U[:, 0, :], uv_out)
            qkv_out(1)
            act.wait_ge(qkT_psum, 1)
            nc.scalar.copy(qT[:, :, 0:P], ps[:, 6, :].rearrange("p (h s) -> p h s", h=GRP)).then_inc(qkT_sb, 1)
            nc.scalar.copy(kT[:, 0:P], ps[:, 7, 0:P]).then_inc(qkT_sb, 1)
            act.wait_ge(proj, 3)
            proj_out(1, ps[:, U_BANK[1], :], U[:, 1, :], uv_out)
            for b in range(2):
                act.wait_ge(pooled_psum, 1)
                nc.scalar.copy(pooled[:, 2 * b:2 * b + 2, :], ps[:, 6 + b, :].rearrange("p (g s) -> p g s", g=2)).then_inc(pooled_sb, 1)
            act.wait_ge(mix_psum, 1)
            for g in range(NG):
                nc.scalar.activation(mixP[:, g, :], ps[:, 4 + g // 2, 256 * (g % 2):256 * (g % 2) + 256], ACT.Copy, scale=scl[:, g:g + 1]).then_inc(mix_sb, 1)
            act.wait_ge(qkT_psum, 2)
            nc.scalar.copy(qT[:, :, P:SEQ], ps[:, 6, :].rearrange("p (h s) -> p h s", h=GRP)).then_inc(qkT_sb, 1)
            nc.scalar.copy(kT[:, P:SEQ], ps[:, 7, 0:P]).then_inc(qkT_sb, 1)

            def softmax_exp(r):
                heads = NQ if r == 0 else NQ // 2
                keys = 1024 // heads
                act.wait_ge(maxed, r + 1)
                for j in range(heads):
                    pr = PR[:, r % 2, j * keys:(j + 1) * keys]
                    nc.scalar.activation(pr, pr, ACT.Exp, bias=nm[:, j:j + 1], accum_out=sm[:, j:j + 1]).then_inc(exped, 1)
                nc.scalar.activation(es[:, 0:heads], es[:, 0:heads], ACT.Exp).then_inc(exped, 1)

            def pt_out(r):
                act.wait_ge(PT_psum, r + 1)
                if r == 1:
                    act.wait_ge(mix_psum, 1)
                nc.scalar.copy(PT[:, r % 2, 0:512], ps[:, SET[r][0], :]).then_inc(PT_a, 1)

            softmax_exp(0)
            pt_out(0)
            softmax_exp(1)
            pt_out(1)
            softmax_exp(2)
            pt_out(2)

            for t in range(T):
                act.wait_ge(h_sb, t + 1)
                if t == 0:
                    act.wait_ge(probs, 3)
                    act.wait_ge(PT_psum, 3)
                nc.scalar.activation(PR[:, t, :], X[:, t, :], ACT.Square, accum_out=nrm[:, t:t + 1]).then_inc(h_ss, 1)
            for t in range(T):
                act.wait_ge(n2T_psum, t + 1)
                nc.scalar.copy(tT[:, 0:4, t * P:(t + 1) * P], ps[:, ACC[t], :].rearrange("p (k s) -> p k s", k=4)).then_inc(n2T_a, 1)
            act.wait_ge(top_in, 1)
            for t in range(T):
                nc.scalar.activation(gts[:, t, 0:TOPK], top[:, t, 0:TOPK], ACT.Exp, bias=lm[:, t:t + 1],
                                     accum_out=gsum[:, t, 0:1]).then_inc(top_exp, 1)
            act.wait_ge(GdT_psum, 1)
            nc.scalar.copy(GdT, ps[0:NE, DWN, 0:T * P].rearrange("p (t s) -> p t s", t=T)).then_inc(GdT_sb, 1)
            act.wait_ge(gathered, 1)
            nc.scalar.copy(xe, ps[:, GAT, :].rearrange("p (k s) -> p k s", k=KC)).then_inc(xe_sb, 1)

            def expert(n):
                for b in range(2):
                    act.wait_ge(g_ready, 2 * n + b + 1)
                    nc.scalar.activation(sg[:, b, :], gb[:, b, :], ACT.Sigmoid, scale=ALPHA).then_inc(sig_ready, 1)
                act.wait_ge(gathered, n + 2)
                nc.scalar.copy(xe, ps[:, GAT, :].rearrange("p (k s) -> p k s", k=KC)).then_inc(xe_sb, 1)
                act.wait_ge(gt_psum, n + 1)
                nc.scalar.copy(GT, ps[:, GAT, 0:T * P].rearrange("p (t s) -> p t s", t=T)).then_inc(gt_sb, 1)
                act.wait_ge(pieces_used, n * PIECES + PIECES)
                nc.scalar.copy(ye, ps[:, DWN, :]).then_inc(y_sb, 1)

            with act.Fori(0, NE) as e:
                expert(e)
            more_passes(act, lambda p, e: expert(p * NE + e))

        @block.vector
        def _(dve):
            steps = [0]

            def link(ins):
                steps[0] += 1
                ins.then_inc(dv, 1)
                dve.wait_ge(dv, steps[0])

            def rsqrt(y, v, t, width):
                link(nc.vector.tensor_scalar(y.bitcast(I32), v.bitcast(I32), 1, None, ALU.logical_shift_right))
                link(nc.vector.tensor_scalar(y.bitcast(I32), y.bitcast(I32), -1.0, RSQRT_MAGIC, ALU.mult, ALU.add))
                for _ in range(3):
                    link(nc.vector.tensor_tensor(t, y, y, ALU.mult))
                    link(nc.vector.scalar_tensor_tensor(t, t, -0.5, v, ALU.mult, ALU.mult))
                    link(nc.vector.scalar_tensor_tensor(y, t, 1.5, y, ALU.add, ALU.mult))

            dve.wait_ge(ld_c, 32)
            for n in range(2 * T):
                t, b = n // 2, n % 2
                dve.wait_ge(xT_psum, n + 1)
                nc.vector.tensor_tensor(tT[:, 4 * b:4 * b + 4, t * P:(t + 1) * P],
                                        ps[:, 6 + b, :].rearrange("p (k s) -> p k s", k=4),
                                        w1c[:, 4 * b:4 * b + 4].unsqueeze(2).to_broadcast([P, 4, P]),
                                        ALU.mult).then_inc(xT_sb, 1)
            dve.wait_ge(x_ss, T)
            link(nc.vector.tensor_scalar(nrm, nrm, 1.0 / DM, EPS, ALU.mult, ALU.add))
            rsqrt(rc[:, 0:T], nrm, rt[:, 0:T], T)
            nc.vector.tensor_copy(rc[:, 4:5], rc[:, 0:1]).then_inc(rstd1, 1)

            dve.wait_ge(ld_small, 16 * 7)
            link(nc.vector.tensor_copy(posf, posi.bitcast(I32)))
            for t in range(T):
                for f in range(2):
                    link(nc.vector.tensor_scalar(trig[:, t, f, :], C[:, C_FREQ:C_FREQ + HALF], posf[:, t:t + 1], None, ALU.mult))
            for f in range(2):
                link(nc.vector.tensor_scalar(turn[:, :, f, :], trig[:, :, f, :], TWO_PI_INV, 0.25 * f, ALU.mult, ALU.add))
            link(nc.vector.tensor_scalar(turn, turn, ROUND, None, ALU.add))
            link(nc.vector.tensor_scalar(turn, turn, ROUND, None, ALU.subtract))
            tf, af = (v.rearrange("p t f h -> p (t f h)") for v in (turn, trig))
            for part in (PI_A, PI_B, PI_C):
                link(nc.vector.scalar_tensor_tensor(af, tf, -part, af, ALU.mult, ALU.add))
            for f in range(2):
                link(nc.vector.tensor_scalar(trig[:, :, f, :], trig[:, :, f, :], f * float(np.pi / 2), SIN_MAX, ALU.add, ALU.min))
            nc.vector.tensor_scalar(tf, af, -SIN_MAX, None, ALU.max).then_inc(trig_arg, 1)

            def norm_rope(t):
                heads = qk[:, t, :].rearrange("p (h d) -> p h d", d=HD)
                sq = tmp[:, 0:QKW].rearrange("p (h d) -> p h d", d=HD)
                dve.wait_ge(qk_out, 3 * t + 3)
                link(nc.vector.tensor_tensor(sq, heads, heads, ALU.mult))
                link(nc.vector.tensor_reduce(ss, sq, AX_X, ALU.add))
                link(nc.vector.tensor_scalar(ss, ss, 1.0 / HD, QK_EPS, ALU.mult, ALU.add))
                rsqrt(rs, ss, rt, NH)
                link(nc.vector.tensor_tensor(heads, heads, rs.unsqueeze(2).to_broadcast([P, NH, HD]), ALU.mult))
                for w, a, b in ((qnw, 0, NQ), (knw, NQ, NH)):
                    link(nc.vector.tensor_tensor(heads[:, a:b, :], heads[:, a:b, :], w.unsqueeze(1).to_broadcast([P, b - a, HD]), ALU.mult))
                pair = heads[:, :, 0:2 * HALF].rearrange("p h (f d) -> p h f d", f=2)
                by_cos = tmp[:, 640:640 + 16 * NH].rearrange("p (h f d) -> p h f d", h=NH, f=2)
                by_sin = tmp[:, 800:800 + 16 * NH].rearrange("p (h f d) -> p h f d", h=NH, f=2)
                if t == 0:
                    dve.wait_ge(trig_done, 1)
                for f, dst in ((1, by_cos), (0, by_sin)):
                    table = trig[:, t, f, :].unsqueeze(1).unsqueeze(1).to_broadcast([P, NH, 2, HALF])
                    link(nc.vector.tensor_tensor(dst, pair, table, ALU.mult))
                nc.vector.tensor_tensor(pair[:, :, 0, :], by_cos[:, :, 0, :], by_sin[:, :, 1, :], ALU.subtract)
                nc.vector.tensor_tensor(pair[:, :, 1, :], by_cos[:, :, 1, :], by_sin[:, :, 0, :], ALU.add).then_inc(roped, 1)
                dve.wait_ge(roped, t + 1)

            def softmax_in(r):
                heads = NQ if r == 0 else NQ // 2
                keys = 1024 // heads
                half = heads // 2
                dve.wait_ge(scores, r + 1)
                mask = C[:, C_MASK + 2 * P - keys:C_MASK + 2 * P].unsqueeze(1).to_broadcast([P, half, keys])
                for g in range(NKV):
                    link(nc.vector.scalar_tensor_tensor(
                        PR[:, r % 2, 512 * g:512 * g + 512].rearrange("p (h k) -> p h k", h=half),
                        ps[:, SET[r][g], :].rearrange("p (h k) -> p h k", h=half),
                        HD ** -0.5, mask, ALU.mult, ALU.add))
                link(nc.vector.tensor_reduce(mx[:, 0:heads], PR[:, r % 2, :].rearrange("p (h k) -> p h k", h=heads), AX_X, ALU.max))
                first = 0 if r < 2 else 2
                sk = sink.rearrange("p (g h) -> p g h", g=NKV)[:, :, first:first + half]
                mg, eg = (v[:, 0:heads].rearrange("p (g h) -> p g h", g=NKV) for v in (mx, es))
                link(nc.vector.tensor_tensor(mg, mg, sk, ALU.max))
                link(nc.vector.tensor_tensor(eg, sk, mg, ALU.subtract))
                nc.vector.tensor_scalar(nm[:, 0:heads], mx[:, 0:heads], -1.0, None, ALU.mult).then_inc(maxed, 1)

            def softmax_out(r):
                heads = NQ if r == 0 else NQ // 2
                keys = 1024 // heads
                dve.wait_ge(exped, (0, 9, 14)[r] + heads + 1)
                link(nc.vector.tensor_tensor(sm[:, 0:heads], sm[:, 0:heads], es[:, 0:heads], ALU.add))
                link(nc.vector.reciprocal(rc[:, 0:heads], sm[:, 0:heads]))
                pr = PR[:, r % 2, :].rearrange("p (h k) -> p h k", h=heads)
                nc.vector.tensor_tensor(pr, pr, rc[:, 0:heads].unsqueeze(2).to_broadcast([P, heads, keys]), ALU.mult).then_inc(probs, 1)

            def pt_out(r):
                dve.wait_ge(PT_psum, r + 1)
                if r == 1:
                    dve.wait_ge(mix_psum, 1)
                nc.vector.tensor_copy(PT[:, r % 2, 512:1024], ps[:, SET[r][1], :]).then_inc(PT_v, 1)

            def ot_out(r):
                dve.wait_ge(oT_psum, r + 1)
                a, n, s = ((0, GRP, 0), (0, 2, P), (2, 2, P))[r]
                nc.vector.tensor_copy(mixA[:, a:a + n, s:s + P],
                                      ps[:, SET[r][0], 0:n * P].rearrange("p (h s) -> p h s", h=n)).then_inc(oT_sb, 1)

            def h_out(t):
                dve.wait_ge(h_psum, t + 1)
                nc.vector.tensor_tensor(X[:, t, :], X[:, t, :], ps[:, ACC[t]:ACC[t] + 2, :].rearrange("p b n -> p (b n)"), ALU.add).then_inc(h_sb, 1)

            def norm2(t):
                dve.wait_ge(h_ss, t + 1)
                link(nc.vector.tensor_scalar(nrm[:, t:t + 1], nrm[:, t:t + 1], 1.0 / DM, EPS, ALU.mult, ALU.add))
                rsqrt(rc[:, t:t + 1], nrm[:, t:t + 1], rt[:, t:t + 1], 1)
                if t == 0:
                    dve.wait_ge(ld_w2, 16)
                nc.vector.scalar_tensor_tensor(N2[:, t, :], X[:, t, :], rc[:, t:t + 1], w2b, ALU.mult, ALU.mult).then_inc(n2_sb, 1)

            norm_rope(0)
            norm_rope(1)
            softmax_in(0)
            softmax_out(0)
            pt_out(0)
            softmax_in(1)
            ot_out(0)
            softmax_out(1)
            softmax_in(2)
            pt_out(1)
            ot_out(1)
            softmax_out(2)
            h_out(0)
            pt_out(2)
            ot_out(2)
            dve.wait_ge(probs, 3)
            norm2(0)
            h_out(1)
            norm2(1)
            for t in range(T):
                dve.wait_ge(n2T_psum, t + 1)
                nc.vector.tensor_copy(tT[:, 4:8, t * P:(t + 1) * P],
                                      ps[:, ACC[t] + 1, :].rearrange("p (k s) -> p k s", k=4)).then_inc(n2T_v, 1)

            dve.wait_ge(logits, T)
            link(nc.vector.tensor_tensor(lg, ps[:, GAT, 0:T * NE].rearrange("p (t e) -> p t e", t=T),
                                         brt.unsqueeze(1).to_broadcast([P, T, NE]), ALU.add))
            for t in range(T):
                link(nc.vector.max(top[:, t, :], lg[:, t, :]))
            nc.vector.tensor_scalar(lm.unsqueeze(2), top[:, :, 0:1], -1.0, None, ALU.mult).then_inc(top_in, 1)
            for t in range(T):
                link(nc.vector.max_index(topi[:, t, :].bitcast(U32), top[:, t, :], lg[:, t, :]))
            link(nc.vector.tensor_copy(idf, topi.bitcast(U32)))
            for j in range(TOPK):
                for t in range(T):
                    if j == 0:
                        ins = nc.vector.tensor_scalar(sel[:, t, :], iota[:, 0:NE], idf[:, t, 0:1], None, ALU.is_equal)
                    else:
                        ins = nc.vector.scalar_tensor_tensor(sel[:, t, :], iota[:, 0:NE], idf[:, t, j:j + 1], sel[:, t, :], ALU.is_equal, ALU.add)
                    link(ins)
            nc.vector.tensor_copy(cnt, sel[:, 0, 0:1]).then_inc(gates, 1)
            dve.wait_ge(top_exp, T)
            link(nc.vector.reciprocal(gsum[:, :, 1:2], gsum[:, :, 0:1]))
            link(nc.vector.tensor_tensor(gts[:, :, 0:TOPK], gts[:, :, 0:TOPK], gsum[:, :, 1:2].to_broadcast([P, T, TOPK]), ALU.mult))
            for j in range(TOPK):
                for t in range(T):
                    dst = Gd if j == 0 else rk
                    link(nc.vector.tensor_scalar(dst[:, t, :], iota[:, 0:NE], idf[:, t, j:j + 1], gts[:, t, j:j + 1], ALU.is_equal, ALU.mult))
                if j:
                    link(nc.vector.tensor_tensor(Gd, Gd, rk, ALU.add))
            nc.vector.tensor_copy(gate[:, :, 0:NE], Gd).then_inc(gates, 1)

            dve.wait_ge(ranks, 1)
            link(nc.vector.scalar_tensor_tensor(rk, ps[:, GAT, 64:64 + T * NE].rearrange("p (t e) -> p t e", t=T), 1.0, sel, ALU.add, ALU.mult))
            for p in range(PASSES + 1):
                last = nc.vector.tensor_scalar(rank[:, :, p * NE:(p + 1) * NE], rk, -1.0 - p * SLOTS, None, ALU.add)
                if p:
                    nc.vector.tensor_copy(gate[:, :, p * NE:(p + 1) * NE], Gd)
            link(last)
            link(nc.vector.tensor_reduce(cnt, ps[:, GAT, 128:128 + NE], AX_X, ALU.max))
            link(nc.vector.tensor_copy(cnti.bitcast(I32), cnt))
            nc.vector.tensor_copy(cnt, cnti.bitcast(I32)).then_inc(count_ready, 1)

            def build_s(n):
                for t in range(T):
                    ins = nc.vector.tensor_scalar(S1[:, t, :], iota[:, 0:SLOTS], rank[:, t, bass.ds(n, 1)], None, ALU.is_equal)
                ins.then_inc(s_ready, 1)

            def build_sg(n):
                for t in range(T):
                    ins = nc.vector.tensor_scalar(SG[:, t, :], iota, rank[:, t, bass.ds(n, 1)], gate[:, t, bass.ds(n, 1)], ALU.is_equal, ALU.mult)
                ins.then_inc(sg_ready, 1)

            def build_oneh(e):
                nc.vector.tensor_scalar(oneh, ones[:, 0:SLOTS], ident[:, bass.ds(e, 1)], None, ALU.mult).then_inc(oneh_ready, 1)

            build_s(0)
            build_sg(0)
            build_oneh(0)
            gu = ps[:, GU:GU + 2, :].rearrange("p b (f n) -> p b f n", f=2)

            def expert(n, e):
                dve.wait_ge(gathered, n + 1)
                build_s(n + 1)
                dve.wait_ge(gu_done, n + 1)
                for b in range(2):
                    nc.vector.tensor_scalar(gb[:, b, :], gu[:, b, 0, :], LIMIT, None, ALU.min).then_inc(g_ready, 1)
                for b in range(2):
                    nc.vector.tensor_scalar(ub[:, b, :], gu[:, b, 1, :], LIMIT, -LIMIT, ALU.min, ALU.max).then_inc(u_ready, 1)
                dve.wait_ge(u_ready, 2 * n + 2)
                dve.wait_ge(g_ready, 2 * n + 2)
                for b in range(2):
                    nc.vector.scalar_tensor_tensor(ub[:, b, :], ub[:, b, :], 1.0, gb[:, b, :], ALU.add, ALU.mult).then_inc(ug_ready, 1)
                for b in range(2):
                    dve.wait_ge(ug_ready, 2 * n + b + 1)
                    dve.wait_ge(sig_ready, 2 * n + b + 1)
                    nc.vector.tensor_tensor(ab[:, b, :], ub[:, b, :], sg[:, b, :], ALU.mult).then_inc(act_ready, 1)
                build_oneh((e + 1) % NE)
                dve.wait_ge(aT_psum, 2 * n + 2)
                nc.vector.tensor_copy(aT, ps[:, DWN, :].rearrange("p (f s) -> p f s", f=4)).then_inc(aT_sb, 1)
                dve.wait_ge(gt_psum, n + 1)
                build_sg(n + 1)

            with dve.Fori(0, NE) as e:
                expert(e, e)
            more_passes(dve, lambda p, e: expert(p * NE + e, e))

            dve.wait_ge(acc_final, 1)
            for t in range(T):
                nc.vector.tensor_tensor(X[:, t, :], X[:, t, :], ps[:, ACC[t]:ACC[t] + 2, :].rearrange("p b n -> p (b n)"), ALU.add).then_inc(out_sb, 1)

        @block.tensor
        def _(pe):
            mm = nc.tensor.matmul
            pe.wait_ge(ld_c, 32)
            for n in range(2 * T):
                t, b = n // 2, n % 2
                if b == 0:
                    pe.wait_ge(ld_x[t], 16)
                if n >= 2:
                    pe.wait_ge(xT_sb, n - 1)
                for k in range(4):
                    kc = 4 * b + k
                    last = nc.tensor.transpose(ps[:, 6 + b, k * P:(k + 1) * P], X[:, t, kc * P:(kc + 1) * P], ident)
                last.then_inc(xT_psum, 1)

            def project(t, parts):
                for k in range(KC):
                    if t == 0:
                        pe.wait_ge(ld_win[k], 16)
                    for bank, a, w in parts:
                        last = mm(ps[:, bank, 0:w], tT[:, k, t * P:(t + 1) * P], win[:, k, a:a + w], start=k == 0, stop=k == KC - 1)
                last.then_inc(proj, 1)

            def qkv(t):
                return [(Q_BANK[t], 0, ATT), (KV_BANK[t], ATT, 2 * VW)]

            def pool_in(t):
                return [(U_BANK[t], QKW + VW, PW)]

            pe.wait_ge(xT_sb, 2)
            project(0, qkv(0) + pool_in(0))
            pe.wait_ge(xT_sb, 4)
            project(1, qkv(1))

            def transpose_qk(t):
                for h in range(GRP):
                    nc.tensor.transpose(ps[:, 6, h * P:(h + 1) * P], qk[:, t, h * P:(h + 1) * P], ident)
                nc.tensor.transpose(ps[:, 7, 0:P], qk[:, t, ATT:QKW], ident).then_inc(qkT_psum, 1)

            def score(r):
                t = 0 if r == 0 else 1
                keys = P if r == 0 else SEQ
                heads = range(GRP) if r == 0 else range(2 * r - 2, 2 * r)
                for n, h in enumerate(heads):
                    for g in range(NKV):
                        rows = slice(g * HD, (g + 1) * HD)
                        last = mm(ps[:, SET[r][g], n * keys:(n + 1) * keys], qT[rows, h, t * P:(t + 1) * P], kT[rows, 0:keys],
                                  start=True, stop=True)
                last.then_inc(scores, 1)

            def transpose_probs(r):
                pe.wait_ge(probs, r + 1)
                for j in range(8):
                    last = nc.tensor.transpose(ps[:, SET[r][j // 4], (j % 4) * P:(j % 4 + 1) * P], PR[:, r % 2, j * P:(j + 1) * P], ident)
                last.then_inc(PT_psum, 1)

            def attend(r):
                pe.wait_ge(PT_a, r + 1)
                pe.wait_ge(PT_v, r + 1)
                blocks = 1 if r == 0 else 2
                n = 4 // blocks
                for kb in range(blocks):
                    for g in range(NKV):
                        pt = PT[:, r % 2, 512 * g:512 * g + 512].rearrange("p (h k q) -> p h k q", h=n, k=blocks)
                        last = mm(ps[g * HD:(g + 1) * HD, SET[r][0], 0:n * P].rearrange("p (h q) -> p h q", h=n), V[:, kb, g * HD:(g + 1) * HD], pt[:, :, kb, :],
                                  start=kb == 0, stop=kb == blocks - 1)
                last.then_inc(oT_psum, 1)

            def out_project(t, src, first):
                for h in range(4):
                    for c in range(2):
                        last = mm(ps[:, ACC[t] + c, :], src[:, h, t * P:(t + 1) * P], wout[:, first + h, 512 * c:512 * c + 512],
                                  start=first == GRP and h == 0, stop=first == 0 and h == 3)
                return last

            pe.wait_ge(roped, 1)
            transpose_qk(0)
            pe.wait_ge(uv_out, 2)
            project(1, pool_in(1))
            pe.wait_ge(qk_out, 3)
            pe.wait_ge(qkT_sb, 2)
            score(0)
            pe.wait_ge(ld_bands, 32)
            pe.wait_ge(uv_out, 4)
            for g in range(NG):
                o = ps[:, 6 + g // 2, 256 * (g % 2):256 * (g % 2) + SEQ]
                mm(o[:, 0:P], U[:, 0, g * P:(g + 1) * P], band[:, g, 0:P], start=True, stop=True)
                mm(o[:, P:SEQ], U[:, 0, g * P:(g + 1) * P], band[:, g, P:SEQ], start=True, stop=False)
                last = mm(o[:, P:SEQ], U[:, 1, g * P:(g + 1) * P], band[:, g, SEQ:SEQ + P], start=False, stop=True)
            last.then_inc(pooled_psum, 1)
            pe.wait_ge(qk_out, 6)
            for g in range(NG):
                if g % 2 == 0:
                    pe.wait_ge(pooled_sb, g // 2 + 1)
                last = mm(ps[:, 4 + g // 2, 256 * (g % 2):256 * (g % 2) + SEQ], poolw[:, g, :], pooled[:, g, :], start=True, stop=True)
            last.then_inc(mix_psum, 1)
            pe.wait_ge(roped, 2)
            transpose_qk(1)
            pe.wait_ge(ld_wout, 48)
            pe.wait_ge(mix_sb, 4)
            out_project(0, mixP, GRP)
            transpose_probs(0)
            pe.wait_ge(qkT_sb, 4)
            score(1)
            attend(0)
            out_project(1, mixP, GRP).then_inc(pool_used, 1)
            pe.wait_ge(oT_sb, 1)
            score(2)
            out_project(0, mixA, 0).then_inc(h_psum, 1)
            transpose_probs(1)
            attend(1)
            transpose_probs(2)
            attend(2)
            pe.wait_ge(oT_sb, 3)
            out_project(1, mixA, 0).then_inc(h_psum, 1)
            for t in range(T):
                pe.wait_ge(n2_sb, t + 1)
                for k in range(KC):
                    last = nc.tensor.transpose(ps[:, ACC[t] + k // 4, (k % 4) * P:(k % 4 + 1) * P], N2[:, t, k * P:(k + 1) * P], ident)
                last.then_inc(n2T_psum, 1)
            pe.wait_ge(ld_small, 16 * 7)
            for t in range(T):
                pe.wait_ge(n2T_a, t + 1)
                pe.wait_ge(n2T_v, t + 1)
                for k in range(KC):
                    last = mm(ps[:, GAT, t * NE:(t + 1) * NE], tT[:, k, t * P:(t + 1) * P], wr[:, k, :], start=k == 0, stop=k == KC - 1)
                last.then_inc(logits, 1)
            pe.wait_ge(gates, 1)
            mm(ps[:, GAT, 64:96], tri, sel[:, 0, :], start=True, stop=True)
            mm(ps[:, GAT, 96:128], ones, sel[:, 0, :], start=True, stop=False)
            mm(ps[:, GAT, 96:128], tri, sel[:, 1, :], start=False, stop=True)
            mm(ps[:, GAT, 128:160], ones, sel[:, 0, :], start=True, stop=False)
            mm(ps[:, GAT, 128:160], ones, sel[:, 1, :], start=False, stop=True).then_inc(ranks, 1)
            pe.wait_ge(gates, 2)
            for t in range(T):
                last = nc.tensor.transpose(ps[0:NE, DWN, t * P:(t + 1) * P], Gd[:, t, :], ident)
            last.then_inc(GdT_psum, 1)

            def gather(n):
                pe.wait_ge(s_ready, n + 1)
                for k in range(KC):
                    for t in range(T):
                        last = mm(ps[:, GAT, k * SLOTS:(k + 1) * SLOTS], N2[:, t, k * P:(k + 1) * P], S1[:, t, :], start=t == 0, stop=t == T - 1)
                last.then_inc(gathered, 1)

            pe.wait_ge(count_ready, 1)
            gather(0)
            pe.wait_ge(GdT_sb, 1)
            pe.wait_ge(ld_bdn, 16)
            for t in range(T):
                for c in range(2):
                    mm(ps[:, ACC[t] + c, :], GdT[:, t, :], bdn[:, 512 * c:512 * c + 512], start=True, stop=True)
            pe.wait_ge(ld_bgu, 16)

            def expert(n):
                def piece(c, chunks):
                    return ring[:, c * PIECE:(c + 1) * PIECE].rearrange("p (k n) -> p k n", k=chunks)

                def gate_up(lhs, rhs, start, stop):
                    cols = rhs.rearrange("p (f n) -> p f n", f=2)
                    for b in range(2):
                        for j in range(2):
                            a = 512 * j + 256 * b
                            last = mm(ps[64 * j:64 * j + 64, GU + b, :].rearrange("p (f n) -> p f n", f=2), lhs, cols[:, :, a:a + 256],
                                      start=start, stop=stop)
                    return last

                pe.wait_ge(xe_sb, n + 1)
                for c in range(GU_PIECES):
                    pe.wait_ge(landed[c], n * 16 + 16)
                    for k in range(2):
                        last = gate_up(xe[:, 2 * c + k, :], piece(c, 2)[:, k, :], c + k == 0, False)
                    last.then_inc(pieces_used, 1)
                pe.wait_ge(oneh_ready, n + 1)
                gate_up(oneh, bgu[:, :], False, True).then_inc(gu_done, 1)

                gather(n + 1)
                for b in range(2):
                    pe.wait_ge(act_ready, n * 2 + b + 1)
                    for c in range(2):
                        last = nc.tensor.transpose(ps[:, DWN, (2 * b + c) * P:(2 * b + c + 1) * P], ab[:, b, c * P:(c + 1) * P], ident)
                    last.then_inc(aT_psum, 1)
                pe.wait_ge(xe_sb, n + 2)
                pe.wait_ge(sg_ready, n + 1)
                for t in range(T):
                    last = nc.tensor.transpose(ps[:, GAT, t * P:(t + 1) * P], SG[:, t, :], ident)
                last.then_inc(gt_psum, 1)

                pe.wait_ge(aT_sb, n + 1)
                for c in range(GU_PIECES, PIECES):
                    pe.wait_ge(landed[c], n * 16 + 16)
                    for k in range(4):
                        for j in range(2):
                            last = mm(ps[64 * j:64 * j + 64, DWN, :], aT[:, k, 64 * (c - GU_PIECES):64 * (c - GU_PIECES) + 64],
                                      piece(c, 4)[:, k, 512 * j:512 * j + 512],
                                      start=c == GU_PIECES and k == 0, stop=c == PIECES - 1 and k == 3)
                    last.then_inc(pieces_used, 1)

                pe.wait_ge(gt_sb, n + 1)
                pe.wait_ge(y_sb, n + 1)
                for t in range(T):
                    for j in range(2):
                        rows = slice(64 * j, 64 * j + 64)
                        mm(ps[:, ACC[t] + j, :], GT[rows, t, :], ye[rows, :], start=False, stop=True, skip_group_check=True)

            with pe.Fori(0, NE) as e:
                expert(e)
            more_passes(pe, lambda p, e: expert(p * NE + e))
            pe.drain().then_inc(acc_final, 1)


_INS = ["x", "positions", "norm1_w", "w_in", "q_norm_w", "k_norm_w", "sinks", "pool_w", "pool_scale", "w_out",
        "norm2_w", "w_router", "b_router", "w_gu", "b_gu", "w_down", "b_down"]


def kernel(**inputs):
    import concourse.bacc as bacc
    from concourse.bass_utils import run_bass_kernel_spmd

    nc = bacc.Bacc("TRN2", target_bir_lowering=False, num_devices=1)
    arrays = {f"{name}_dram": np.ascontiguousarray(inputs[name]) for name in _INS}
    arrays["consts_dram"], arrays["bands_dram"] = shape_constants()
    args = [nc.dram_tensor(name, a.shape, mybir.dt.from_np(a.dtype), kind="ExternalInput").ap() for name, a in arrays.items()]
    out = nc.dram_tensor("out_dram", arrays["x_dram"].shape, F32, kind="ExternalOutput").ap()
    layer_kernel(nc, *args, out)
    r = run_bass_kernel_spmd(nc, [arrays], core_ids=[0])
    return r.results[0]["out_dram"]
```

```python
from contextlib import ExitStack

import numpy as np
import concourse.bass as bass
from concourse import mybir

F32 = mybir.dt.float32
I32 = mybir.dt.int32
U32 = mybir.dt.uint32
BF16 = mybir.dt.bfloat16
ALU = mybir.AluOpType
ACT = mybir.ActivationFunctionType
AX_X = mybir.AxisListType.X

P = 128
SEQ, DM = 256, 1024
T = SEQ // P
KC = DM // P
HD = 64
NQ, NKV = 8, 2
NH = NQ + NKV
GRP = NQ // NKV
QKW = NH * HD
ATT = NQ * HD
VW = NKV * HD
PW = DM - ATT
INW = QKW + VW + PW
WINDOW = 128
HALF = HD // 4 // 2
POOLS = (2, 4, 8, 16)
NG = len(POOLS)
NE, TOPK, FF = 32, 4, 1024
LIMIT, ALPHA = 7.0, 1.702
EPS, QK_EPS = 1e-5, 1e-6
NEG = -1e30
SLOTS = 64
PASSES = SEQ // SLOTS
PIECES = 6
GU_PIECES = 4
RING = 8
TURN = 4
TURNS = NE // TURN
TP = TURN * PIECES
PIECE = 4096
ROUNDS = 3
NR = NE * (PASSES + 1)

C_ID, C_TRI, C_ONE, C_MASK, C_IOTA, C_FREQ, C_PASS, C_EXP = 0, 128, 256, 384, 640, 768, 776, 936
NC_COLS = C_EXP + NE

TWO_PI_INV = float(np.float32(1.0 / (2.0 * np.pi)))
PI_A = 6.28125
PI_B = float(np.float32(np.float32((2.0 * np.pi - PI_A) * 2.0**21).round() / 2.0**21))
PI_C = float(np.float32(2.0 * np.pi - PI_A - PI_B))
ROUND = 12582912.0
SIN_MAX = 3.1415925
RSQRT_MAGIC = 1597463007.0


def shape_constants():
    c = np.zeros((P, NC_COLS), np.float32)
    i = np.arange(P)
    c[:, C_ID:C_ID + P] = np.eye(P)
    c[:, C_TRI:C_TRI + P] = i[:, None] < i[None, :]
    c[:, C_ONE:C_ONE + P] = 1.0
    c[:, C_MASK:C_MASK + P] = np.where(i[None, :] > i[:, None] + P - WINDOW, 0.0, NEG)
    c[:, C_MASK + P:C_MASK + 2 * P] = np.where(i[None, :] <= i[:, None], 0.0, NEG)
    c[:, C_IOTA:C_IOTA + P] = np.tile(np.arange(SLOTS), P // SLOTS)[None, :]
    c[:, C_FREQ:C_FREQ + HALF] = np.float32(500000.0) ** (-np.arange(0, 2 * HALF, 2, dtype=np.float32) / (2 * HALF))
    c[:, C_PASS:C_EXP] = -1.0 - SLOTS * np.repeat(np.arange(PASSES + 1), NE)[None, :]
    c[:, C_EXP:NC_COLS] = i[:, None] % NE == np.arange(NE)[None, :]
    bands = np.zeros((P, NG, SEQ + P), np.float32)
    s = np.arange(SEQ)
    for g, w in enumerate(POOLS):
        full = ((s[:, None] <= s[None, :]) & (s[:, None] > s[None, :] - w)) / np.minimum(s + 1, w)[None, :] - np.eye(SEQ)
        bands[:, g, :SEQ] = full[:P]
        bands[:, g, SEQ:] = full[P:, P:]
    return c, bands.reshape(P, NG * (SEQ + P))


def layer_kernel(nc, x, positions, norm1_w, w_in, q_norm_w, k_norm_w, sinks, pool_w, pool_scale,
                 w_out, norm2_w, w_router, b_router, w_gu, b_gu, w_down, b_down, consts, bands, out):
    x_t = x.rearrange("b (t p) d -> p (b t) d", p=P)
    out_t = out.rearrange("b (t p) d -> (b t) p d", p=P)
    w_in_k = w_in.rearrange("(k p) n -> p k n", p=P)
    w_out_a = w_out[0:ATT, :].rearrange("(g h d) n -> g d h n", g=NKV, d=HD)
    w_out_p = w_out[ATT:DM, :].rearrange("(k p) n -> p k n", p=P)
    w_gu_k = w_gu.rearrange("e (k p) n -> p (e k) n", p=P)
    w_dn_k = w_down.rearrange("e (k p) n -> p (e k) n", p=P)

    with ExitStack() as ctx:
        def sb(name, shape, dt=F32):
            return ctx.enter_context(nc.sbuf_tensor(name, shape, dt))

        def sem(name):
            return ctx.enter_context(nc.semaphore(name))

        ring = sb("ring", [P, RING * PIECE])
        X = sb("X", [P, T, DM])
        N2 = sb("N2", [P, T, DM])
        bgs = sb("bgs", [3 * NE, 2 * FF], BF16)
        tT = sb("tT", [P, KC, SEQ])
        qk = sb("qk", [P, T, QKW])
        U = sb("U", [P, T, PW])
        V = sb("V", [P, T, VW])
        qT = sb("qT", [P, GRP, SEQ])
        kT = sb("kT", [P, SEQ])
        PR = sb("PR", [P, 2, 1024])
        PT = sb("PT", [P, 2, 1024])
        mixA = sb("mixA", [P, GRP, SEQ])
        mixP = sb("mixP", [P, NG, SEQ])
        C = sb("C", [P, NC_COLS])
        wr = sb("wr", [P, KC, NE])
        small = sb("small", [P, 544])
        spare = sb("spare", [P, 2, 512])
        tri, ones = (sb(name, [P, P], BF16) for name in ("tri", "ones"))
        sel = sb("sel", [P, T, NE], BF16)

        front = ring[:, 3 * PIECE:6 * PIECE]
        win = front[:, 0:KC * INW].rearrange("p (k n) -> p k n", k=KC)
        band = front[:, KC * INW:KC * INW + NG * (SEQ + P)].rearrange("p (g s) -> p g s", g=NG)
        poolw = front[:, KC * INW + NG * (SEQ + P):3 * PIECE].rearrange("p (g n) -> p g n", g=NG)
        wout = ring[:, 6 * PIECE:8 * PIECE].rearrange("p (k n) -> p k n", k=KC)
        pooled = PT[:, 1, :].rearrange("p (g s) -> p g s", g=NG)
        w2b = U[:, :, :].rearrange("p t n -> p (t n)")
        bdn = mixP[:, :, :].rearrange("p g s -> p (g s)")[0:NE, :]
        tmp = PR[:, 1, :]

        def block_of(buf):
            return buf.rearrange("p (f n) -> p f n", f=2)

        ahead = [spare[:, :, :], block_of(mixA[:, :, :].rearrange("p h s -> p (h s)")), block_of(PR[:, 0, :]),
                 block_of(qT[:, :, :].rearrange("p h s -> p (h s)")), block_of(X[:, 0, :]), block_of(w2b),
                 block_of(X[:, 1, :]), block_of(PR[:, 1, :])]

        ident = C[:, C_ID:C_ID + P]
        iota = C[:, C_IOTA:C_IOTA + P]

        at = [0]

        def cut(n, of=small):
            at[0] += n
            return of[:, at[0] - n:at[0]]

        w1c, w2c = cut(KC), cut(KC)
        scl = cut(NG)
        qnw, knw = cut(HD), cut(HD)
        sink = cut(NQ)
        brt = cut(NE)
        posi, posf = cut(T), cut(T)
        trig = cut(T * 2 * HALF).rearrange("p (t f h) -> p t f h", t=T, f=2)
        turn = cut(T * 2 * HALF).rearrange("p (t f h) -> p t f h", t=T, f=2)
        ss, rs, rt = cut(NH), cut(NH), cut(NH)
        nrm, rms = cut(T), cut(T)
        mx, nm, es, sm, rc = cut(8), cut(8), cut(8), cut(8), cut(8)
        lg, lm = cut(T * NE).rearrange("p (t e) -> p t e", t=T), cut(T)
        top, gts, gsum = (cut(T * 8).rearrange("p (t e) -> p t e", t=T) for _ in range(3))
        cnt, cnti = cut(1), cut(1)
        assert at[0] <= 544

        at[0] = 0
        of = tT[:, :, :].rearrange("p k s -> p (k s)")
        gb, sg, ub, ab = (cut(512, of).rearrange("p (b n) -> p b n", b=2) for _ in range(4))
        at[0] = 0
        of = PT[:, :, :].rearrange("p r s -> p (r s)")
        xe = cut(KC * SLOTS, of).rearrange("p (k s) -> p k s", k=KC)
        aT = cut(512, of).rearrange("p (f s) -> p f s", f=4)
        ye = cut(512, of)
        GT = cut(T * P, of).rearrange("p (t s) -> p t s", t=T)
        GdT = cut(T * P, of).rearrange("p (t s) -> p t s", t=T)[0:NE]
        at[0] = 0
        of = qk[:, :, :].rearrange("p t n -> p (t n)")
        S1 = cut(T * SLOTS, of).rearrange("p (t s) -> p t s", t=T)
        SG = cut(T * P, of).rearrange("p (t s) -> p t s", t=T)
        rank = cut(T * NR, of).rearrange("p (t e) -> p t e", t=T)
        gate = cut(T * NR, of).rearrange("p (t e) -> p t e", t=T)
        rk = cut(T * NE, of).rearrange("p (t e) -> p t e", t=T)
        oneh = sb("oneh", [3 * NE, SLOTS], BF16)

        at[0] = 0
        route = PR[:, 1, :]
        Gd = cut(T * NE, route).rearrange("p (t e) -> p t e", t=T)
        hot, hotg = (cut(T * TOPK * NE, route).rearrange("p (t j e) -> p t j e", t=T, j=TOPK) for _ in range(2))
        topi = cut(T * 8, route).rearrange("p (t e) -> p t e", t=T)
        squares = (qk[:, :, :].rearrange("p t n -> p (t n)")[:, 0:DM], qT[:, :, :].rearrange("p h s -> p (h s)"))

        ps = ctx.enter_context(nc.psum_tensor("ps", [P, 8, 512], F32))
        Q_BANK, U_BANK, KV_BANK = (0, 3), (2, 4), (1, 5)
        SET = ((0, 1), (6, 7), (0, 1))
        ACC = (2, 4)
        POOLED, MIXED = (3, 5), (2, 4)
        RANKS, LOGITS = 6, 7
        GU, GAT, DWN = 6, 0, 1

        ld_x = [sem(f"ld_x{t}") for t in range(T)]
        ld_id, ld_c, ld_small, ld_bands = sem("ld_id"), sem("ld_c"), sem("ld_small"), sem("ld_bands")
        ld_win = [sem(f"ld_win{k}") for k in range(KC)]
        ld_winu = sem("ld_winu")
        landed_last = [sem(f"landed_last{k}") for k in range(KC)]
        ld_ahead = [sem(f"ld_ahead{u}") for u in range(TURN)]
        ld_wout, ld_w2, ld_bdn, ld_bgu = sem("ld_wout"), sem("ld_w2"), sem("ld_bdn"), sem("ld_bgu")
        landed = [sem(f"landed{c}") for c in range(RING)]
        split = sem("split")
        stored = sem("stored")
        dv = sem("dv")
        x_ss = sem("x_ss")
        xT_psum, xT_sb, proj = sem("xT_psum"), sem("xT_sb"), sem("proj")
        weighed = sem("weighed")
        rstd1, rstd2 = sem("rstd1"), sem("rstd2")
        trig_arg, trig_done = sem("trig_arg"), sem("trig_done")
        qk_out, uv_out, roped = sem("qk_out"), sem("uv_out"), sem("roped")
        qkT_psum, qkT_sb = sem("qkT_psum"), sem("qkT_sb")
        scores, maxed, exped, probs = sem("scores"), sem("maxed"), sem("exped"), sem("probs")
        PT_psum, PT_a, PT_v = sem("PT_psum"), sem("PT_a"), sem("PT_v")
        oT_psum, oT_sb = sem("oT_psum"), sem("oT_sb")
        pooled_psum, pooled_sb, mix_psum, mix_sb = sem("pooled_psum"), sem("pooled_sb"), sem("mix_psum"), sem("mix_sb")
        pool_used = sem("pool_used")
        h_psum, h_sb, h_ss, n2_sb = sem("h_psum"), sem("h_sb"), sem("h_ss"), sem("n2_sb")
        opened, order_ready = sem("opened"), sem("order_ready")
        hT_psum, hT_a, hT_v, logits = sem("hT_psum"), sem("hT_a"), sem("hT_v"), sem("logits")
        top_in, top_exp, gates = sem("top_in"), sem("top_exp"), sem("gates")
        picked, wr_ready = sem("picked"), sem("wr_ready")
        ranks, GdT_psum, GdT_sb, count_ready = sem("ranks"), sem("GdT_psum"), sem("GdT_sb"), sem("count_ready")
        pieces_used = sem("pieces_used")
        s_ready, sg_ready, oneh_ready = sem("s_ready"), sem("sg_ready"), sem("oneh_ready")
        gathered, xe_sb = sem("gathered"), sem("xe_sb")
        gu_done, gu_free, g_ready, sig_ready, act_ready = sem("gu_done"), sem("gu_free"), sem("g_ready"), sem("sig_ready"), sem("act_ready")
        u_ready, ug_ready = sem("u_ready"), sem("ug_ready")
        aT_psum, aT_sb = sem("aT_psum"), sem("aT_sb")
        gt_psum, gt_sb, y_sb = sem("gt_psum"), sem("gt_sb"), sem("y_sb")
        acc_final, out_a, out_v = sem("acc_final"), sem("out_a"), sem("out_v")

        block = ctx.enter_context(nc.Block())

        def more_passes(eng, count, body):
            eng.wait_ge(count_ready, 1)
            most = eng.value_load(cnti[0:1, 0:1].bitcast(I32), min_val=0, max_val=SEQ)
            with eng.If(most > SLOTS):
                with eng.Fori(1, PASSES) as p:
                    with eng.Fori(0, count) as e:
                        body(p, e)

        @block.sync
        def _(sp):
            for t in range(T):
                sp.dma_start(X[:, t, :], x_t[:, t, :]).then_inc(ld_x[t], 16)
            for k in range(KC):
                sp.dma_start(win[:, k, 0:QKW + VW], w_in_k[:, k, 0:QKW + VW]).then_inc(ld_win[k], 16)
            for k in range(0, KC, 4):
                sp.dma_start(win[:, k:k + 4, QKW + VW:INW], w_in_k[:, k:k + 4, QKW + VW:INW]).then_inc(ld_winu, 16)
            sp.dma_start(band, bands.rearrange("p (g s) -> p g s", g=NG)).then_inc(ld_bands, 16)
            sp.dma_start(poolw, pool_w.rearrange("g c d -> c g d")).then_inc(ld_bands, 16)
            sp.dma_start(wout[:, 0:NG, :], w_out_p).then_inc(ld_wout, 16)
            for g in range(NKV):
                sp.dma_start(wout[g * HD:(g + 1) * HD, NG:KC, :], w_out_a[g]).then_inc(ld_wout, 16)

            def load_piece(s, first=0, skip=0):
                slot, e, c = s % RING, first + s // PIECES, s % PIECES
                if c < GU_PIECES:
                    chunks, row, src = 2, 2 * c, w_gu_k
                else:
                    chunks, row, src = 4, 4 * (c - GU_PIECES), w_dn_k
                dst = ring[:, slot * PIECE:(slot + 1) * PIECE].rearrange("p (k n) -> p k n", k=chunks)
                sp.dma_start(dst[:, skip:, :], src[:, bass.ds(e * KC + row + skip, chunks - skip), :]).then_inc(landed[slot], 16)

            def load_ahead(n):
                src = w_gu_k[:, (NE - 2 * TURN + n // 2) * KC, :].rearrange("p (f j n) -> p j f n", f=2, j=2)
                sp.dma_start(ahead[n], src[:, n % 2]).then_inc(ld_ahead[n // 2], 16)

            for s in range(3):
                load_piece(s)
            sp.wait_ge(proj, 4)
            for s in range(3, 5):
                load_piece(s)
            sp.wait_ge(mix_psum, 1)
            load_piece(5)
            load_ahead(0)
            sp.dma_start(w2b, norm2_w.rearrange("(a n) -> a n", a=1).to_broadcast([P, DM])).then_inc(ld_w2, 16)
            sp.wait_ge(pool_used, 1)
            load_piece(6)
            sp.dma_start(bdn, b_down).then_inc(ld_bdn, 16)
            sp.wait_ge(h_psum, 2 * T)
            load_piece(7)
            for n in range(1, 3):
                load_ahead(n)
            sp.wait_ge(h_ss, T)
            load_ahead(3)
            sp.wait_ge(opened, 1)
            sp.wait_ge(n2_sb, 1)
            load_ahead(4)
            sp.wait_ge(n2_sb, T)
            load_ahead(5)
            sp.wait_ge(opened, T)
            load_ahead(6)
            sp.wait_ge(GdT_psum, 1)
            sp.wait_ge(sg_ready, 1)
            load_ahead(7)

            with sp.Fori(0, TURNS - 3) as r:
                for s in range(TP):
                    sp.wait_ge(pieces_used, r * TP + s + 1)
                    load_piece(RING + s, r * TURN)
            for s in range(RING, 3 * TP):
                sp.wait_ge(pieces_used, (TURNS - 3) * TP + s - RING + 1)
                if s < 3 * TP - 2:
                    load_piece(s, NE - 3 * TURN, skip=1 if s // TP == 1 and s % PIECES == 0 else 0)
                else:
                    for k in range(4):
                        f = 4 * (s - (3 * TP - 2)) + k
                        sp.dma_start(ring[:, s % RING * PIECE + k * DM:s % RING * PIECE + (k + 1) * DM],
                                     w_dn_k[:, (NE - 1) * KC + f, :]).then_inc(landed_last[f], 16)

            def next_pass(p, r):
                for s in range(TP):
                    sp.wait_ge(pieces_used, p * (NE * PIECES) + r * TP + (s + 1 - RING))
                    load_piece(s, r * TURN)

            more_passes(sp, TURNS, next_pass)

            for t in range(T):
                for c, done in enumerate((out_v, out_a)):
                    sp.wait_ge(done, t + 1)
                    sp.dma_start(out_t[t][:, 512 * c:512 * c + 512], X[:, t, 512 * c:512 * c + 512]).then_inc(stored, 16)
            sp.wait_ge(stored, 16 * T * 2)

        @block.gpsimd
        def _(pool):
            pool.wait_ge(ld_small, 16 * 9)
            nc.gpsimd.tensor_copy(tri[:, :], C[:, C_TRI:C_TRI + P]).then_inc(order_ready, 1)
            nc.gpsimd.tensor_copy(ones[:, :], C[:, C_ONE:C_ONE + P]).then_inc(order_ready, 1)
            f = N2[0:3 * NE, :, :].rearrange("p t n -> p (t n)")
            pool.wait_ge(ld_bgu, 48)
            nc.gpsimd.tensor_copy(bgs[:, :], f).then_inc(split, 1)
            for n in range(1, 3):
                rows = slice(0, (3 - n) * NE)
                pool.wait_ge(split, 2 * n - 1)
                nc.gpsimd.tensor_tensor(f[rows], f[rows], bgs[rows, :], ALU.subtract).then_inc(split, 1)
                pool.wait_ge(split, 2 * n)
                nc.gpsimd.tensor_copy(bgs[rows, :], f[rows]).then_inc(split, 1)
            pool.wait_ge(split, 5)
            pool.wait_ge(ld_w2, 16)
            pool.wait_ge(h_sb, 2 * T)
            nc.gpsimd.tensor_tensor(N2[:, 1, :], X[:, 1, :], w2b, ALU.mult).then_inc(weighed, 1)

        @block.scalar
        def _(act):
            act.dma_start(ident, consts[:, C_ID:C_ID + P]).then_inc(ld_id, 16)
            act.dma_start(w1c, norm1_w.rearrange("(k p) -> p k", p=P), allow_slow_non_contiguous=True).then_inc(ld_c, 16)
            act.dma_start(posi.bitcast(I32), positions.rearrange("b (t p) -> p (b t)", p=P), allow_slow_non_contiguous=True).then_inc(ld_small, 16)
            act.dma_start(scl, pool_scale.rearrange("(g p) -> p g", p=P), allow_slow_non_contiguous=True).then_inc(ld_small, 16)
            act.dma_start(w2c, norm2_w.rearrange("(k p) -> p k", p=P), allow_slow_non_contiguous=True).then_inc(ld_small, 16)
            for dst, src in ((qnw, q_norm_w), (knw, k_norm_w), (sink, sinks), (brt, b_router)):
                row = src.rearrange("(a n) -> a n", a=1)
                act.dma_start(dst, row.to_broadcast([P, row.shape[1]])).then_inc(ld_small, 16)
            act.dma_start(C[:, C_TRI:NC_COLS], consts[:, C_TRI:NC_COLS]).then_inc(ld_small, 16)
            act.dma_start(wr[:, :, :], w_router.rearrange("(k p) e -> p k e", p=P)).then_inc(ld_small, 16)
            for n in range(3):
                act.dma_start(N2[n * NE:(n + 1) * NE, :, :].rearrange("p t n -> p (t n)"), b_gu).then_inc(ld_bgu, 16)

            for t in range(T):
                act.wait_ge(ld_x[t], 16)
                nc.scalar.activation(PR[:, t, :], X[:, t, :], ACT.Square, accum_out=nrm[:, t:t + 1]).then_inc(x_ss, 1)
            act.wait_ge(trig_arg, 1)
            nc.scalar.activation(trig, turn, ACT.Sin).then_inc(trig_done, 1)

            def proj_out(t, src, dst, s):
                nc.scalar.activation(dst, src, ACT.Copy, scale=rms[:, t:t + 1]).then_inc(s, 1)

            def qkv_out(t):
                act.wait_ge(proj, t + 1)
                for g in range(NKV):
                    proj_out(t, ps[:, Q_BANK[t], g * GRP * HD:(g + 1) * GRP * HD].rearrange("p (h d) -> p h d", h=GRP),
                             qk[:, t, 0:ATT].rearrange("p (h g d) -> p g h d", g=NKV, h=GRP)[:, g], qk_out)
                proj_out(t, ps[:, KV_BANK[t], 0:VW], qk[:, t, ATT:QKW], qk_out)
                proj_out(t, ps[:, KV_BANK[t], VW:2 * VW], V[:, t, :], uv_out)

            def u_out(t):
                act.wait_ge(proj, 2 + t + 1)
                proj_out(t, ps[:, U_BANK[t], :], U[:, t, :], uv_out)

            def qkT_out(t):
                act.wait_ge(qkT_psum, t + 1)
                nc.scalar.copy(qT[:, :, t * P:(t + 1) * P], ps[:, 6, :].rearrange("p (h s) -> p h s", h=GRP)).then_inc(qkT_sb, 1)
                nc.scalar.copy(kT[:, t * P:(t + 1) * P], ps[:, 7, 0:P]).then_inc(qkT_sb, 1)

            def softmax_exp(r):
                heads = NQ if r == 0 else NQ // 2
                keys = 1024 // heads
                act.wait_ge(maxed, r + 1)
                for j in range(heads):
                    pr = PR[:, r % 2, j * keys:(j + 1) * keys]
                    nc.scalar.activation(pr, pr, ACT.Exp, bias=nm[:, j:j + 1], accum_out=sm[:, j:j + 1]).then_inc(exped, 1)
                nc.scalar.activation(es[:, 0:heads], es[:, 0:heads], ACT.Exp).then_inc(exped, 1)

            def pt_out(r):
                act.wait_ge(PT_psum, r + 1)
                nc.scalar.copy(PT[:, r % 2, 0:512], ps[:, SET[r][0], :]).then_inc(PT_a, 1)

            act.wait_ge(rstd1, 1)
            qkv_out(0)
            qkv_out(1)
            qkT_out(0)
            u_out(0)
            softmax_exp(0)
            u_out(1)
            qkT_out(1)
            for b, bank in enumerate(POOLED):
                act.wait_ge(pooled_psum, 1)
                nc.scalar.copy(pooled[:, 2 * b:2 * b + 2, :], ps[:, bank, :].rearrange("p (g s) -> p g s", g=2)).then_inc(pooled_sb, 1)
            pt_out(0)
            act.wait_ge(mix_psum, 1)
            for g in range(NG):
                nc.scalar.activation(mixP[:, g, :], ps[:, MIXED[g // 2], 256 * (g % 2):256 * (g % 2) + 256], ACT.Copy,
                                     scale=scl[:, g:g + 1]).then_inc(mix_sb, 1)
            softmax_exp(1)
            pt_out(1)
            softmax_exp(2)
            pt_out(2)

            for t in range(T):
                act.wait_ge(h_sb, 2 * t + 2)
                nc.scalar.activation(squares[t], X[:, t, :], ACT.Square, accum_out=nrm[:, t:t + 1]).then_inc(h_ss, 1)
                act.wait_ge(hT_psum, 2 * t + 1)
                nc.scalar.copy(tT[:, 0:4, t * P:(t + 1) * P], ps[:, ACC[t], :].rearrange("p (k s) -> p k s", k=4)).then_inc(hT_a, 1)
                if t == 1:
                    act.wait_ge(weighed, 1)
                    act.wait_ge(rstd2, T)
                    nc.scalar.activation(N2[:, 1, :], N2[:, 1, :], ACT.Copy, scale=rms[:, 1:2]).then_inc(n2_sb, 1)
                act.wait_ge(top_in, t + 1)
                nc.scalar.activation(gts[:, t, 0:TOPK], top[:, t, 0:TOPK], ACT.Exp, bias=lm[:, t:t + 1],
                                     accum_out=gsum[:, t, 0:1]).then_inc(top_exp, 1)
            act.wait_ge(gathered, 1)
            nc.scalar.copy(xe, ps[:, GAT, :].rearrange("p (k s) -> p k s", k=KC)).then_inc(xe_sb, 1)
            act.wait_ge(GdT_psum, 1)
            nc.scalar.copy(GdT, ps[0:NE, DWN, 0:T * P].rearrange("p (t s) -> p t s", t=T)).then_inc(GdT_sb, 1)

            def expert(n):
                for b in range(2):
                    act.wait_ge(g_ready, 2 * n + b + 1)
                    nc.scalar.activation(sg[:, b, :], gb[:, b, :], ACT.Sigmoid, scale=ALPHA).then_inc(sig_ready, 1)
                act.wait_ge(gathered, n + 2)
                nc.scalar.copy(xe, ps[:, GAT, :].rearrange("p (k s) -> p k s", k=KC)).then_inc(xe_sb, 1)
                act.wait_ge(gt_psum, n + 1)
                nc.scalar.copy(GT, ps[:, GAT, 0:T * P].rearrange("p (t s) -> p t s", t=T)).then_inc(gt_sb, 1)
                act.wait_ge(pieces_used, n * PIECES + PIECES)
                nc.scalar.copy(ye, ps[:, DWN, :]).then_inc(y_sb, 1)

            with act.Fori(0, NE) as e:
                expert(e)
            more_passes(act, NE, lambda p, e: expert(p * NE + e))

            act.wait_ge(acc_final, 1)
            for t in range(T):
                nc.scalar.copy(X[:, t, 512:1024], ps[:, ACC[t] + 1, :]).then_inc(out_a, 1)

        @block.vector
        def _(dve):
            steps = [0]

            def link(ins):
                steps[0] += 1
                ins.then_inc(dv, 1)
                dve.wait_ge(dv, steps[0])

            def rsqrt(y, v, t):
                link(nc.vector.tensor_scalar(y.bitcast(I32), v.bitcast(I32), 1, None, ALU.logical_shift_right))
                link(nc.vector.tensor_scalar(y.bitcast(I32), y.bitcast(I32), -1.0, RSQRT_MAGIC, ALU.mult, ALU.add))
                for n in range(3):
                    link(nc.vector.tensor_tensor(t, y, y, ALU.mult))
                    link(nc.vector.scalar_tensor_tensor(t, t, -0.5, v, ALU.mult, ALU.mult))
                    last = nc.vector.scalar_tensor_tensor(y, t, 1.5, y, ALU.add, ALU.mult)
                    if n < 2:
                        link(last)
                return last

            dve.wait_ge(ld_c, 16)
            for n in range(2 * T):
                t, b = n // 2, n % 2
                dve.wait_ge(xT_psum, n + 1)
                nc.vector.tensor_tensor(tT[:, 4 * b:4 * b + 4, t * P:(t + 1) * P],
                                        ps[:, 6 + b, :].rearrange("p (k s) -> p k s", k=4),
                                        w1c[:, 4 * b:4 * b + 4].unsqueeze(2).to_broadcast([P, 4, P]),
                                        ALU.mult).then_inc(xT_sb, 1)
            dve.wait_ge(x_ss, T)
            link(nc.vector.tensor_scalar(nrm, nrm, 1.0 / DM, EPS, ALU.mult, ALU.add))
            rsqrt(rms, nrm, rt[:, 0:T]).then_inc(rstd1, 1)

            dve.wait_ge(ld_small, 16 * 9)
            link(nc.vector.tensor_copy(posf, posi.bitcast(I32)))
            for t in range(T):
                for f in range(2):
                    link(nc.vector.tensor_scalar(trig[:, t, f, :], C[:, C_FREQ:C_FREQ + HALF], posf[:, t:t + 1], None, ALU.mult))
            for f in range(2):
                link(nc.vector.tensor_scalar(turn[:, :, f, :], trig[:, :, f, :], TWO_PI_INV, 0.25 * f, ALU.mult, ALU.add))
            link(nc.vector.tensor_scalar(turn, turn, ROUND, None, ALU.add))
            link(nc.vector.tensor_scalar(turn, turn, ROUND, None, ALU.subtract))
            tf, af = (v.rearrange("p t f h -> p (t f h)") for v in (turn, trig))
            for part in (PI_A, PI_B, PI_C):
                link(nc.vector.scalar_tensor_tensor(af, tf, -part, af, ALU.mult, ALU.add))
            for f in range(2):
                link(nc.vector.tensor_scalar(trig[:, :, f, :], trig[:, :, f, :], f * float(np.pi / 2), SIN_MAX, ALU.add, ALU.min))
            nc.vector.tensor_scalar(tf, af, -SIN_MAX, None, ALU.max).then_inc(trig_arg, 1)

            def norm_rope(t):
                heads = qk[:, t, :].rearrange("p (h d) -> p h d", d=HD)
                sq = tmp[:, 0:QKW].rearrange("p (h d) -> p h d", d=HD)
                dve.wait_ge(qk_out, 3 * t + 3)
                link(nc.vector.tensor_tensor(sq, heads, heads, ALU.mult))
                link(nc.vector.tensor_reduce(ss, sq, AX_X, ALU.add))
                link(nc.vector.tensor_scalar(ss, ss, 1.0 / HD, QK_EPS, ALU.mult, ALU.add))
                link(rsqrt(rs, ss, rt))
                link(nc.vector.tensor_tensor(heads, heads, rs.unsqueeze(2).to_broadcast([P, NH, HD]), ALU.mult))
                for w, a, b in ((qnw, 0, NQ), (knw, NQ, NH)):
                    link(nc.vector.tensor_tensor(heads[:, a:b, :], heads[:, a:b, :], w.unsqueeze(1).to_broadcast([P, b - a, HD]), ALU.mult))
                pair = heads[:, :, 0:2 * HALF].rearrange("p h (f d) -> p h f d", f=2)
                by_cos = tmp[:, 640:640 + 16 * NH].rearrange("p (h f d) -> p h f d", h=NH, f=2)
                by_sin = tmp[:, 800:800 + 16 * NH].rearrange("p (h f d) -> p h f d", h=NH, f=2)
                if t == 0:
                    dve.wait_ge(trig_done, 1)
                for f, dst in ((1, by_cos), (0, by_sin)):
                    table = trig[:, t, f, :].unsqueeze(1).unsqueeze(1).to_broadcast([P, NH, 2, HALF])
                    link(nc.vector.tensor_tensor(dst, pair, table, ALU.mult))
                nc.vector.tensor_tensor(pair[:, :, 0, :], by_cos[:, :, 0, :], by_sin[:, :, 1, :], ALU.subtract)
                nc.vector.tensor_tensor(pair[:, :, 1, :], by_cos[:, :, 1, :], by_sin[:, :, 0, :], ALU.add).then_inc(roped, 1)
                dve.wait_ge(roped, t + 1)

            def softmax_in(r):
                heads = NQ if r == 0 else NQ // 2
                keys = 1024 // heads
                half = heads // 2
                dve.wait_ge(scores, r + 1)
                mask = C[:, C_MASK + 2 * P - keys:C_MASK + 2 * P].unsqueeze(1).to_broadcast([P, half, keys])
                for g in range(NKV):
                    link(nc.vector.scalar_tensor_tensor(
                        PR[:, r % 2, 512 * g:512 * g + 512].rearrange("p (h k) -> p h k", h=half),
                        ps[:, SET[r][g], :].rearrange("p (h k) -> p h k", h=half),
                        HD ** -0.5, mask, ALU.mult, ALU.add))
                link(nc.vector.tensor_reduce(mx[:, 0:heads], PR[:, r % 2, :].rearrange("p (h k) -> p h k", h=heads), AX_X, ALU.max))
                first = 0 if r < 2 else 2
                sk = sink.rearrange("p (g h) -> p g h", g=NKV)[:, :, first:first + half]
                mg, eg = (v[:, 0:heads].rearrange("p (g h) -> p g h", g=NKV) for v in (mx, es))
                link(nc.vector.tensor_tensor(mg, mg, sk, ALU.max))
                link(nc.vector.tensor_tensor(eg, sk, mg, ALU.subtract))
                nc.vector.tensor_scalar(nm[:, 0:heads], mx[:, 0:heads], -1.0, None, ALU.mult).then_inc(maxed, 1)

            def softmax_out(r):
                heads = NQ if r == 0 else NQ // 2
                keys = 1024 // heads
                dve.wait_ge(exped, (0, 9, 14)[r] + heads + 1)
                link(nc.vector.tensor_tensor(sm[:, 0:heads], sm[:, 0:heads], es[:, 0:heads], ALU.add))
                link(nc.vector.reciprocal(rc[:, 0:heads], sm[:, 0:heads]))
                pr = PR[:, r % 2, :].rearrange("p (h k) -> p h k", h=heads)
                nc.vector.tensor_tensor(pr, pr, rc[:, 0:heads].unsqueeze(2).to_broadcast([P, heads, keys]), ALU.mult).then_inc(probs, 1)

            def pt_out(r):
                dve.wait_ge(PT_psum, r + 1)
                if r == 1:
                    dve.wait_ge(mix_psum, 1)
                nc.vector.tensor_copy(PT[:, r % 2, 512:1024], ps[:, SET[r][1], :]).then_inc(PT_v, 1)

            def ot_out(r):
                dve.wait_ge(oT_psum, r + 1)
                a, n, s = ((0, GRP, 0), (0, 2, P), (2, 2, P))[r]
                nc.vector.tensor_copy(mixA[:, a:a + n, s:s + P],
                                      ps[:, SET[r][0], 0:n * P].rearrange("p (h s) -> p h s", h=n)).then_inc(oT_sb, 1)

            def h_out(t):
                for c in range(2):
                    dve.wait_ge(h_psum, 2 * t + c + 1)
                    half = X[:, t, 512 * c:512 * c + 512]
                    nc.vector.tensor_tensor(half, half, ps[:, ACC[t] + c, :], ALU.add).then_inc(h_sb, 1)

            def rms2(t):
                dve.wait_ge(h_ss, t + 1)
                link(nc.vector.tensor_scalar(nrm[:, t:t + 1], nrm[:, t:t + 1], 1.0 / DM, EPS, ALU.mult, ALU.add))
                rsqrt(rms[:, t:t + 1], nrm[:, t:t + 1], rt[:, t:t + 1]).then_inc(rstd2, 1)
                dve.wait_ge(rstd2, t + 1)

            def hT_out(t):
                dve.wait_ge(hT_psum, 2 * t + 2)
                nc.vector.tensor_copy(tT[:, 4:8, t * P:(t + 1) * P],
                                      ps[:, ACC[t] + 1, :].rearrange("p (k s) -> p k s", k=4)).then_inc(hT_v, 1)

            def pick(t):
                dve.wait_ge(logits, t + 1)
                link(nc.vector.scalar_tensor_tensor(lg[:, t, :], ps[:, LOGITS, t * NE:(t + 1) * NE], rms[:, t:t + 1], brt, ALU.mult, ALU.add))
                link(nc.vector.max(top[:, t, :], lg[:, t, :]))
                nc.vector.tensor_scalar(lm[:, t:t + 1], top[:, t, 0:1], -1.0, None, ALU.mult).then_inc(top_in, 1)
                link(nc.vector.max_index(topi[:, t, :].bitcast(U32), top[:, t, :], lg[:, t, :]))
                link(nc.vector.tensor_tensor(hot[:, t], iota[:, 0:NE].unsqueeze(1).to_broadcast([P, TOPK, NE]),
                                             topi[:, t, 0:TOPK].bitcast(U32).unsqueeze(2).to_broadcast([P, TOPK, NE]), ALU.is_equal))
                with nc.allow_low_precision(reason="at most one of a token's four is an expert: the sum is 0 or 1"):
                    nc.vector.tensor_reduce(sel[:, t, :], hot[:, t].rearrange("p j e -> p e j"), AX_X, ALU.add).then_inc(picked, 1)

            def weigh(t):
                dve.wait_ge(top_exp, t + 1)
                link(nc.vector.reciprocal(gsum[:, t, 1:2], gsum[:, t, 0:1]))
                link(nc.vector.tensor_scalar(gts[:, t, 0:TOPK], gts[:, t, 0:TOPK], gsum[:, t, 1:2], None, ALU.mult))
                link(nc.vector.tensor_tensor(hotg[:, t], hot[:, t], gts[:, t, 0:TOPK].unsqueeze(2).to_broadcast([P, TOPK, NE]), ALU.mult))
                nc.vector.tensor_reduce(Gd[:, t, :], hotg[:, t].rearrange("p j e -> p e j"), AX_X, ALU.add).then_inc(gates, 1)

            norm_rope(0)
            norm_rope(1)
            softmax_in(0)
            softmax_out(0)
            pt_out(0)
            softmax_in(1)
            ot_out(0)
            softmax_out(1)
            softmax_in(2)
            nc.vector.tensor_tensor(wr[:, :, :], wr[:, :, :], w2c.unsqueeze(2).to_broadcast([P, KC, NE]), ALU.mult).then_inc(wr_ready, 1)
            pt_out(1)
            softmax_out(2)
            ot_out(1)
            pt_out(2)
            h_out(0)
            ot_out(2)
            hT_out(0)
            rms2(0)
            dve.wait_ge(ld_w2, 16)
            dve.wait_ge(split, 5)
            nc.vector.scalar_tensor_tensor(N2[:, 0, :], X[:, 0, :], rms[:, 0:1], w2b, ALU.mult, ALU.mult).then_inc(n2_sb, 1)
            pick(0)
            weigh(0)
            h_out(1)
            hT_out(1)
            rms2(1)
            pick(1)
            dve.wait_ge(ranks, 1)
            link(nc.vector.scalar_tensor_tensor(rk, ps[:, RANKS, 0:T * NE].rearrange("p (t e) -> p t e", t=T), 1.0, sel[:, :, :], ALU.add, ALU.mult))
            link(nc.vector.tensor_tensor(rank.rearrange("p t (r e) -> p t r e", e=NE),
                                         rk.unsqueeze(2).to_broadcast([P, T, PASSES + 1, NE]),
                                         C[:, C_PASS:C_EXP].rearrange("p (r e) -> p r e", e=NE).unsqueeze(1).to_broadcast([P, T, PASSES + 1, NE]),
                                         ALU.add))

            def build_s(n):
                for t in range(T):
                    ins = nc.vector.tensor_scalar(S1[:, t, :], iota[:, 0:SLOTS], rank[:, t, bass.ds(n, 1)], None, ALU.is_equal)
                ins.then_inc(s_ready, 1)

            def build_sg(n):
                for t in range(T):
                    ins = nc.vector.tensor_scalar(SG[:, t, :], iota, rank[:, t, bass.ds(n, 1)], gate[:, t, bass.ds(n, 1)], ALU.is_equal, ALU.mult)
                ins.then_inc(sg_ready, 1)

            def build_oneh(e):
                nc.vector.tensor_scalar(oneh[:, :], C[0:3 * NE, C_ONE:C_ONE + SLOTS], C[0:3 * NE, bass.ds(e + C_EXP, 1)], None, ALU.mult).then_inc(oneh_ready, 1)

            build_s(0)
            build_oneh(0)
            link(nc.vector.tensor_reduce(cnt, ps[:, RANKS, T * NE:(T + 1) * NE], AX_X, ALU.max))
            nc.vector.tensor_copy(cnti.bitcast(I32), cnt).then_inc(count_ready, 1)
            weigh(1)
            dve.wait_ge(gates, T)
            link(nc.vector.tensor_copy(gate.rearrange("p t (r e) -> p t r e", e=NE), Gd.unsqueeze(2).to_broadcast([P, T, PASSES + 1, NE])))
            build_sg(0)
            gu = ps[:, GU:GU + 2, :].rearrange("p b (f n) -> p b f n", f=2)

            def expert(n, e):
                dve.wait_ge(gathered, n + 1)
                build_s(n + 1)
                dve.wait_ge(gu_done, n + 1)
                for b in range(2):
                    nc.vector.tensor_scalar(gb[:, b, :], gu[:, b, 0, :], LIMIT, None, ALU.min).then_inc(g_ready, 1)
                for b in range(2):
                    nc.vector.tensor_scalar(ub[:, b, :], gu[:, b, 1, :], LIMIT, -LIMIT, ALU.min, ALU.max).then_inc(u_ready, 1)
                dve.wait_ge(u_ready, 2 * n + 2)
                dve.wait_ge(g_ready, 2 * n + 2)
                for b in range(2):
                    nc.vector.scalar_tensor_tensor(ub[:, b, :], ub[:, b, :], 1.0, gb[:, b, :], ALU.add, ALU.mult).then_inc(ug_ready, 1)
                for b in range(2):
                    dve.wait_ge(ug_ready, 2 * n + b + 1)
                    dve.wait_ge(sig_ready, 2 * n + b + 1)
                    nc.vector.tensor_tensor(ab[:, b, :], ub[:, b, :], sg[:, b, :], ALU.mult).then_inc(act_ready, 1)
                build_oneh((e + 1) % NE)
                dve.wait_ge(aT_psum, 2 * n + 2)
                nc.vector.tensor_copy(aT, ps[:, DWN, :].rearrange("p (f s) -> p f s", f=4)).then_inc(aT_sb, 1)
                dve.wait_ge(gt_psum, n + 1)
                build_sg(n + 1)

            with dve.Fori(0, NE) as e:
                expert(e, e)
            more_passes(dve, NE, lambda p, e: expert(p * NE + e, e))

            dve.wait_ge(acc_final, 1)
            for t in range(T):
                nc.vector.tensor_copy(X[:, t, 0:512], ps[:, ACC[t], :]).then_inc(out_v, 1)

        @block.tensor
        def _(pe):
            mm = nc.tensor.matmul
            pe.wait_ge(ld_id, 16)
            for n in range(2 * T):
                t, b = n // 2, n % 2
                if b == 0:
                    pe.wait_ge(ld_x[t], 16)
                if n >= 2:
                    pe.wait_ge(xT_sb, n - 1)
                for k in range(4):
                    kc = 4 * b + k
                    last = nc.tensor.transpose(ps[:, 6 + b, k * P:(k + 1) * P], X[:, t, kc * P:(kc + 1) * P], ident)
                last.then_inc(xT_psum, 1)

            def project(t, parts):
                for k in range(KC):
                    if parts[0][1] == 0:
                        pe.wait_ge(ld_win[k], 16)
                    elif k % 4 == 0:
                        pe.wait_ge(ld_winu, 32)
                    for bank, a, w in parts:
                        last = mm(ps[:, bank, 0:w], tT[:, k, t * P:(t + 1) * P], win[:, k, a:a + w], start=k == 0, stop=k == KC - 1)
                last.then_inc(proj, 1)

            def qkv(t):
                return [(Q_BANK[t], 0, ATT), (KV_BANK[t], ATT, 2 * VW)]

            def pool_in(t):
                return [(U_BANK[t], QKW + VW, PW)]

            pe.wait_ge(xT_sb, 2)
            project(0, qkv(0))
            pe.wait_ge(xT_sb, 4)
            project(1, qkv(1))
            project(0, pool_in(0))

            def transpose_qk(t):
                for h in range(GRP):
                    nc.tensor.transpose(ps[:, 6, h * P:(h + 1) * P], qk[:, t, h * P:(h + 1) * P], ident)
                nc.tensor.transpose(ps[:, 7, 0:P], qk[:, t, ATT:QKW], ident).then_inc(qkT_psum, 1)

            def score(r):
                t = 0 if r == 0 else 1
                keys = P if r == 0 else SEQ
                heads = range(GRP) if r == 0 else range(2 * r - 2, 2 * r)
                for n, h in enumerate(heads):
                    for g in range(NKV):
                        rows = slice(g * HD, (g + 1) * HD)
                        last = mm(ps[:, SET[r][g], n * keys:(n + 1) * keys], qT[rows, h, t * P:(t + 1) * P], kT[rows, 0:keys],
                                  start=True, stop=True)
                last.then_inc(scores, 1)

            def transpose_probs(r):
                pe.wait_ge(probs, r + 1)
                for j in range(8):
                    last = nc.tensor.transpose(ps[:, SET[r][j // 4], (j % 4) * P:(j % 4 + 1) * P], PR[:, r % 2, j * P:(j + 1) * P], ident)
                last.then_inc(PT_psum, 1)

            def attend(r):
                pe.wait_ge(PT_a, r + 1)
                pe.wait_ge(PT_v, r + 1)
                blocks = 1 if r == 0 else 2
                n = 4 // blocks
                for kb in range(blocks):
                    for g in range(NKV):
                        pt = PT[:, r % 2, 512 * g:512 * g + 512].rearrange("p (h k q) -> p h k q", h=n, k=blocks)
                        last = mm(ps[g * HD:(g + 1) * HD, SET[r][0], 0:n * P].rearrange("p (h q) -> p h q", h=n), V[:, kb, g * HD:(g + 1) * HD], pt[:, :, kb, :],
                                  start=kb == 0, stop=kb == blocks - 1)
                last.then_inc(oT_psum, 1)

            def out_project(t, src, first, heads, banks=range(2)):
                for h in heads:
                    for c in banks:
                        last = mm(ps[:, ACC[t] + c, :], src[:, h, t * P:(t + 1) * P], wout[:, first + h, 512 * c:512 * c + 512],
                                  start=first == 0 and h == 0, stop=first == NG and h == GRP - 1)
                return last

            pe.wait_ge(roped, 1)
            transpose_qk(0)
            pe.wait_ge(qk_out, 6)
            pe.wait_ge(uv_out, 2)
            pe.wait_ge(qkT_sb, 2)
            score(0)
            project(1, pool_in(1))
            pe.wait_ge(roped, 2)
            transpose_qk(1)
            pe.wait_ge(ld_bands, 32)
            pe.wait_ge(uv_out, 4)
            for g in range(NG):
                o = ps[:, POOLED[g // 2], 256 * (g % 2):256 * (g % 2) + SEQ]
                mm(o[:, 0:P], U[:, 0, g * P:(g + 1) * P], band[:, g, 0:P], start=True, stop=True)
                mm(o[:, P:SEQ], U[:, 0, g * P:(g + 1) * P], band[:, g, P:SEQ], start=True, stop=False)
                last = mm(o[:, P:SEQ], U[:, 1, g * P:(g + 1) * P], band[:, g, SEQ:SEQ + P], start=False, stop=True)
            last.then_inc(pooled_psum, 1)
            pe.wait_ge(qkT_sb, 4)
            score(1)
            transpose_probs(0)
            for g in range(NG):
                if g % 2 == 0:
                    pe.wait_ge(pooled_sb, g // 2 + 1)
                last = mm(ps[:, MIXED[g // 2], 256 * (g % 2):256 * (g % 2) + SEQ], poolw[:, g, :], pooled[:, g, :], start=True, stop=True)
            last.then_inc(mix_psum, 1)
            attend(0)
            pe.wait_ge(ld_wout, 48)
            pe.wait_ge(mix_sb, 4)
            out_project(0, mixP, 0, range(4))
            pe.wait_ge(oT_sb, 1)
            score(2)
            transpose_probs(1)
            out_project(1, mixP, 0, range(4)).then_inc(pool_used, 1)
            attend(1)
            transpose_probs(2)
            for c in range(2):
                out_project(0, mixA, NG, range(4), [c]).then_inc(h_psum, 1)
            attend(2)

            def transpose_h(t):
                for b in range(2):
                    pe.wait_ge(h_sb, 2 * t + b + 1)
                    for k in range(4):
                        last = nc.tensor.transpose(ps[:, ACC[t] + b, k * P:(k + 1) * P], X[:, t, (4 * b + k) * P:(4 * b + k + 1) * P], ident)
                    last.then_inc(hT_psum, 1)

            def route(t):
                pe.wait_ge(hT_a, t + 1)
                pe.wait_ge(hT_v, t + 1)
                for k in range(KC):
                    last = mm(ps[:, LOGITS, t * NE:(t + 1) * NE], tT[:, k, t * P:(t + 1) * P], wr[:, k, :], start=k == 0, stop=k == KC - 1)
                last.then_inc(logits, 1)

            transpose_h(0)
            pe.wait_ge(oT_sb, 3)
            out_project(1, mixA, NG, range(2))
            pe.wait_ge(wr_ready, 1)
            route(0)
            for c in range(2):
                out_project(1, mixA, NG, range(2, 4), [c]).then_inc(h_psum, 1)

            def open_sums(t, c):
                return mm(ps[:, ACC[t] + c, :], ident, X[:, t, 512 * c:512 * c + 512], start=True, stop=True)

            open_sums(0, 0)
            transpose_h(1)
            open_sums(0, 1).then_inc(opened, 1)
            route(1)
            open_sums(1, 0)
            pe.wait_ge(order_ready, 2)
            pe.wait_ge(picked, T)
            mm(ps[:, RANKS, 0:32], tri[:, :], sel[:, 0, :], start=True, stop=True)
            mm(ps[:, RANKS, 32:64], ones[:, :], sel[:, 0, :], start=True, stop=False)
            mm(ps[:, RANKS, 32:64], tri[:, :], sel[:, 1, :], start=False, stop=True)
            mm(ps[:, RANKS, 64:96], ones[:, :], sel[:, 0, :], start=True, stop=False)
            mm(ps[:, RANKS, 64:96], ones[:, :], sel[:, 1, :], start=False, stop=True).then_inc(ranks, 1)
            open_sums(1, 1).then_inc(opened, 1)

            def gather(n):
                pe.wait_ge(s_ready, n + 1)
                for k in range(KC):
                    for t in range(T):
                        last = mm(ps[:, GAT, k * SLOTS:(k + 1) * SLOTS], N2[:, t, k * P:(k + 1) * P], S1[:, t, :], start=t == 0, stop=t == T - 1)
                last.then_inc(gathered, 1)

            pe.wait_ge(n2_sb, T)
            gather(0)
            pe.wait_ge(gates, T)
            for t in range(T):
                last = nc.tensor.transpose(ps[0:NE, DWN, t * P:(t + 1) * P], Gd[:, t, :], ident)
            last.then_inc(GdT_psum, 1)
            pe.wait_ge(split, 5)
            pe.wait_ge(count_ready, 1)

            def expert(turn, u, step=None):
                n = turn * TURN + u

                def piece(c, chunks):
                    slot = (u * PIECES + c) % RING
                    return ring[:, slot * PIECE:(slot + 1) * PIECE].rearrange("p (k n) -> p k n", k=chunks)

                def wait_landed(c):
                    s = u * PIECES + c
                    less = 16 if step == "more" and s % RING >= RING - 2 else 0
                    pe.wait_ge(landed[s % RING], turn * (16 * TP // RING) + (16 * (s // RING + 1) - less))

                def gate_up(lhs, halves, start, stop):
                    for b in range(2):
                        for j in range(2):
                            last = mm(ps[64 * j:64 * j + 64, GU + b, :].rearrange("p (f n) -> p f n", f=2), lhs,
                                      halves[j][:, :, 256 * b:256 * b + 256], start=start, stop=stop)
                    return last

                def halves_of(row):
                    both = row.rearrange("p (f j n) -> p j f n", f=2, j=2)
                    return both[:, 0], both[:, 1]

                pe.wait_ge(xe_sb, n + 1)
                for c in range(GU_PIECES):
                    if c > 0 or step != "ahead":
                        wait_landed(c)
                    for k in range(2):
                        halves = halves_of(piece(c, 2)[:, k, :])
                        if c + k == 0 and step == "ahead":
                            pe.wait_ge(ld_ahead[u], 32)
                            halves = ahead[2 * u:2 * u + 2]
                        elif c == 0 and step == "ahead":
                            wait_landed(0)
                        last = gate_up(xe[:, 2 * c + k, :], halves, c + k == 0, False)
                    last.then_inc(pieces_used, 1)
                pe.wait_ge(oneh_ready, n + 1)
                gate_up(oneh[:, :], halves_of(bgs[:, :]), False, True).then_inc(gu_done, 1)

                gather(n + 1)
                for b in range(2):
                    pe.wait_ge(act_ready, n * 2 + b + 1)
                    for c in range(2):
                        last = nc.tensor.transpose(ps[:, DWN, (2 * b + c) * P:(2 * b + c + 1) * P], ab[:, b, c * P:(c + 1) * P], ident)
                    last.then_inc(aT_psum, 1)
                pe.wait_ge(xe_sb, n + 2)
                pe.wait_ge(sg_ready, n + 1)
                for t in range(T):
                    last = nc.tensor.transpose(ps[:, GAT, t * P:(t + 1) * P], SG[:, t, :], ident)
                last.then_inc(gt_psum, 1)

                pe.wait_ge(aT_sb, n + 1)
                for c in range(GU_PIECES, PIECES):
                    if step != "last":
                        wait_landed(c)
                    for k in range(4):
                        if step == "last":
                            pe.wait_ge(landed_last[4 * (c - GU_PIECES) + k], 16)
                        for j in range(2):
                            last = mm(ps[64 * j:64 * j + 64, DWN, :], aT[:, k, 64 * (c - GU_PIECES):64 * (c - GU_PIECES) + 64],
                                      piece(c, 4)[:, k, 512 * j:512 * j + 512],
                                      start=c == GU_PIECES and k == 0, stop=c == PIECES - 1 and k == 3)
                    last.then_inc(pieces_used, 1)

                pe.wait_ge(gt_sb, n + 1)
                pe.wait_ge(y_sb, n + 1)
                for t in range(T):
                    for j in range(2):
                        rows = slice(64 * j, 64 * j + 64)
                        mm(ps[:, ACC[t] + j, :], GT[rows, t, :], ye[rows, :], start=False, stop=True, skip_group_check=True)

            with pe.Fori(0, TURNS - 2) as r:
                for u in range(TURN):
                    expert(r, u)
            for u in range(TURN):
                expert(TURNS - 2, u, "ahead")
            pe.wait_ge(ld_bdn, 16)
            pe.wait_ge(GdT_sb, 1)
            for t in range(T):
                for c in range(2):
                    mm(ps[:, ACC[t] + c, :], GdT[:, t, :], bdn[:, 512 * c:512 * c + 512], start=False, stop=True, skip_group_check=True)
            for u in range(TURN):
                expert(TURNS - 1, u, "last" if u == TURN - 1 else None)

            def next_pass(p, r):
                for u in range(TURN):
                    expert(p * TURNS + r, u, "more")

            more_passes(pe, TURNS, next_pass)
            pe.drain().then_inc(acc_final, 1)


_INS = ["x", "positions", "norm1_w", "w_in", "q_norm_w", "k_norm_w", "sinks", "pool_w", "pool_scale", "w_out",
        "norm2_w", "w_router", "b_router", "w_gu", "b_gu", "w_down", "b_down"]


def kernel(**inputs):
    import concourse.bacc as bacc
    from concourse.bass_utils import run_bass_kernel_spmd

    nc = bacc.Bacc("TRN2", target_bir_lowering=False, num_devices=1)
    arrays = {f"{name}_dram": np.ascontiguousarray(inputs[name]) for name in _INS}
    arrays["consts_dram"], arrays["bands_dram"] = shape_constants()
    args = [nc.dram_tensor(name, a.shape, mybir.dt.from_np(a.dtype), kind="ExternalInput").ap() for name, a in arrays.items()]
    out = nc.dram_tensor("out_dram", arrays["x_dram"].shape, F32, kind="ExternalOutput").ap()
    layer_kernel(nc, *args, out)
    r = run_bass_kernel_spmd(nc, [arrays], core_ids=[0])
    return r.results[0]["out_dram"]
```

```python
from contextlib import ExitStack

import numpy as np
import concourse.bass as bass
from concourse import mybir

F32 = mybir.dt.float32
I32 = mybir.dt.int32
U32 = mybir.dt.uint32
BF16 = mybir.dt.bfloat16
ALU = mybir.AluOpType
ACT = mybir.ActivationFunctionType
AX_X = mybir.AxisListType.X

P = 128
SEQ, DM = 256, 1024
T = SEQ // P
KC = DM // P
HD = 64
NQ, NKV = 8, 2
NH = NQ + NKV
GRP = NQ // NKV
QKW = NH * HD
ATT = NQ * HD
VW = NKV * HD
PW = DM - ATT
INW = QKW + VW + PW
WINDOW = 128
HALF = HD // 4 // 2
POOLS = (2, 4, 8, 16)
NG = len(POOLS)
NE, TOPK, FF = 32, 4, 1024
LIMIT, ALPHA = 7.0, 1.702
EPS, QK_EPS = 1e-5, 1e-6
NEG = -1e30
SLOTS = 64
PASSES = SEQ // SLOTS
PIECES = 6
GU_PIECES = 4
RING = 8
TURN = 4
TURNS = NE // TURN
TP = TURN * PIECES
PIECE = 4096
ROUNDS = 3
NR = NE * (PASSES + 1)

AHEAD = 5

C_ID, C_ONE, C_IOTA, C_EXP = 0, P, 2 * P, 3 * P
C_FRONT = C_EXP + NE
C_TRI, C_MASK, C_FREQ = C_FRONT, C_FRONT + P, C_FRONT + 3 * P
C_PASS = C_FREQ + HALF
NC_COLS = C_PASS + NR

TWO_PI_INV = float(np.float32(1.0 / (2.0 * np.pi)))
PI_A = 6.28125
PI_B = float(np.float32(np.float32((2.0 * np.pi - PI_A) * 2.0**21).round() / 2.0**21))
PI_C = float(np.float32(2.0 * np.pi - PI_A - PI_B))
ROUND = 12582912.0
SIN_MAX = 3.1415925
RSQRT_MAGIC = 1597463007.0


def shape_constants():
    c = np.zeros((P, NC_COLS), np.float32)
    i = np.arange(P)
    c[:, C_ID:C_ID + P] = np.eye(P)
    c[:, C_TRI:C_TRI + P] = i[:, None] < i[None, :]
    c[:, C_ONE:C_ONE + P] = 1.0
    c[:, C_MASK:C_MASK + P] = np.where(i[None, :] > i[:, None] + P - WINDOW, 0.0, NEG)
    c[:, C_MASK + P:C_MASK + 2 * P] = np.where(i[None, :] <= i[:, None], 0.0, NEG)
    c[:, C_IOTA:C_IOTA + P] = np.tile(np.arange(SLOTS), P // SLOTS)[None, :]
    c[:, C_FREQ:C_FREQ + HALF] = np.float32(500000.0) ** (-np.arange(0, 2 * HALF, 2, dtype=np.float32) / (2 * HALF))
    c[:, C_PASS:NC_COLS] = -1.0 - SLOTS * np.repeat(np.arange(PASSES + 1), NE)[None, :]
    c[:, C_EXP:C_FRONT] = i[:, None] % NE == np.arange(NE)[None, :]
    bands = np.zeros((P, NG, SEQ + P), np.float32)
    s = np.arange(SEQ)
    for g, w in enumerate(POOLS):
        full = ((s[:, None] <= s[None, :]) & (s[:, None] > s[None, :] - w)) / np.minimum(s + 1, w)[None, :] - np.eye(SEQ)
        bands[:, g, :SEQ] = full[:P]
        bands[:, g, SEQ:] = full[P:, P:]
    return c, bands.reshape(P, NG * (SEQ + P))


def layer_kernel(nc, x, positions, norm1_w, w_in, q_norm_w, k_norm_w, sinks, pool_w, pool_scale,
                 w_out, norm2_w, w_router, b_router, w_gu, b_gu, w_down, b_down, consts, bands, out):
    x_t = x.rearrange("b (t p) d -> p (b t) d", p=P)
    out_t = out.rearrange("b (t p) d -> (b t) p d", p=P)
    w_in_k = w_in.rearrange("(k p) n -> p k n", p=P)
    w_out_a = w_out[0:ATT, :].rearrange("(g h d) n -> g d h n", g=NKV, d=HD)
    w_out_p = w_out[ATT:DM, :].rearrange("(k p) n -> p k n", p=P)
    w_gu_k = w_gu.rearrange("e (k p) n -> p (e k) n", p=P)
    w_dn_k = w_down.rearrange("e (k p) n -> p (e k) n", p=P)

    with ExitStack() as ctx:
        def sb(name, shape, dt=F32):
            return ctx.enter_context(nc.sbuf_tensor(name, shape, dt))

        def sem(name):
            return ctx.enter_context(nc.semaphore(name))

        ring = sb("ring", [P, RING * PIECE])
        X = sb("X", [P, T, DM])
        N2 = sb("N2", [P, T, DM])
        bgs = sb("bgs", [3 * NE, 2 * FF], BF16)
        tT = sb("tT", [P, KC, SEQ])
        qk = sb("qk", [P, T, QKW])
        U = sb("U", [P, T, PW])
        qT = sb("qT", [P, GRP, SEQ])
        PR = sb("PR", [P, 2, 1024])
        PT = sb("PT", [P, 2, 1024])
        mixA = sb("mixA", [P, GRP, SEQ])
        mixP = sb("mixP", [P, NG, SEQ])
        C = sb("C", [P, C_FRONT])
        passing = sb("passing", [P, 2048])
        counts = sb("counts", [P, 2])
        spare = sb("spare", [P, 1024])
        tri, ones = (sb(name, [P, P], BF16) for name in ("tri", "ones"))
        sel = sb("sel", [P, T, NE], BF16)

        front = ring[:, 3 * PIECE:6 * PIECE]
        win = front[:, 0:KC * INW].rearrange("p (k n) -> p k n", k=KC)
        band = front[:, KC * INW:KC * INW + NG * (SEQ + P)].rearrange("p (g s) -> p g s", g=NG)
        poolw = front[:, KC * INW + NG * (SEQ + P):3 * PIECE].rearrange("p (g n) -> p g n", g=NG)
        wout = ring[:, 6 * PIECE:8 * PIECE].rearrange("p (k n) -> p k n", k=KC)
        pooled = PT[:, 1, :].rearrange("p (g s) -> p g s", g=NG)
        w2b = U[:, :, :].rearrange("p t n -> p (t n)")
        bdn = spare[0:NE, :]
        tmp = PR[:, 1, :]

        at = [0]

        def cut(n, of=passing):
            at[0] += n
            return of[:, at[0] - n:at[0]]

        tri32, mask, freq, passed = cut(P), cut(2 * P), cut(HALF), cut(NR)
        V = cut(T * VW).rearrange("p (t n) -> p t n", t=T)
        kT = cut(SEQ)
        wr = cut(KC * NE).rearrange("p (k e) -> p k e", k=KC)
        ident = C[:, C_ID:C_ID + P]
        iota = C[:, C_IOTA:C_IOTA + P]

        w1c, w2c = cut(KC), cut(KC)
        scl = cut(NG)
        qnw, knw = cut(HD), cut(HD)
        sink = cut(NQ)
        brt = cut(NE)
        posi, posf = cut(T), cut(T)
        trig = cut(T * 2 * HALF).rearrange("p (t f h) -> p t f h", t=T, f=2)
        turn = cut(T * 2 * HALF).rearrange("p (t f h) -> p t f h", t=T, f=2)
        ss, rs, rt = cut(NH), cut(NH), cut(NH)
        nrm, rms = cut(T), cut(T)
        mx, nm, es, sm, rc = cut(8), cut(8), cut(8), cut(8), cut(8)
        lg, lm = cut(T * NE).rearrange("p (t e) -> p t e", t=T), cut(T)
        top, gts, gsum = (cut(T * 8).rearrange("p (t e) -> p t e", t=T) for _ in range(3))
        assert at[0] <= 2048
        cnt, cnti = counts[:, 0:1], counts[:, 1:2]

        at[0] = 0
        of = tT[:, :, :].rearrange("p k s -> p (k s)")
        gb, sg, ub, ab = (cut(512, of).rearrange("p (b n) -> p b n", b=2) for _ in range(4))
        at[0] = 0
        of = PT[:, :, :].rearrange("p r s -> p (r s)")
        xe = cut(KC * SLOTS, of).rearrange("p (k s) -> p k s", k=KC)
        aT = cut(512, of).rearrange("p (f s) -> p f s", f=4)
        ye = cut(512, of)
        GT = cut(T * P, of).rearrange("p (t s) -> p t s", t=T)
        GdT = cut(T * P, of).rearrange("p (t s) -> p t s", t=T)[0:NE]
        at[0] = 0
        of = qk[:, :, :].rearrange("p t n -> p (t n)")
        S1 = cut(T * SLOTS, of).rearrange("p (t s) -> p t s", t=T)
        SG = cut(T * P, of).rearrange("p (t s) -> p t s", t=T)
        rank = cut(T * NR, of).rearrange("p (t e) -> p t e", t=T)
        gate = cut(T * NR, of).rearrange("p (t e) -> p t e", t=T)
        rk = cut(T * NE, of).rearrange("p (t e) -> p t e", t=T)
        oneh = sb("oneh", [3 * NE, SLOTS], BF16)

        at[0] = 0
        route = PT[:, 1, :]
        Gd = cut(T * NE, route).rearrange("p (t e) -> p t e", t=T)
        hot, hotg = (cut(T * TOPK * NE, route).rearrange("p (t j e) -> p t j e", t=T, j=TOPK) for _ in range(2))
        topi = cut(T * 8, route).rearrange("p (t e) -> p t e", t=T)
        squares = qk[:, :, :].rearrange("p t n -> p (t n)")[:, 0:DM]

        ahead = [block.rearrange("p (f n) -> p f n", f=2) for block in (
            spare[:, :], qT[:, :, :].rearrange("p h s -> p (h s)"), PR[:, 1, :],
            mixA[:, :, :].rearrange("p h s -> p (h s)"), PR[:, 0, :], X[:, 0, :], w2b, X[:, 1, :],
            passing[:, 0:1024], passing[:, 1024:2048])]
        down_ahead = mixP[:, :, :].rearrange("p g s -> p (g s)")

        ps = ctx.enter_context(nc.psum_tensor("ps", [P, 8, 512], F32))
        Q_BANK, U_BANK, KV_BANK = (0, 3), (2, 4), (1, 5)
        SET = ((0, 1), (6, 7), (0, 1))
        ACC = (2, 4)
        POOLED, MIXED = (3, 5), (2, 4)
        RANKS, LOGITS = 6, 7
        GU, GAT, DWN = 6, 0, 1

        ld_x = [sem(f"ld_x{t}") for t in range(T)]
        ld_id, ld_c, ld_small, ld_late, ld_bands = sem("ld_id"), sem("ld_c"), sem("ld_small"), sem("ld_late"), sem("ld_bands")
        ld_win = [sem(f"ld_win{k}") for k in range(KC)]
        ld_winu = sem("ld_winu")
        landed_last = [sem(f"landed_last{k}") for k in range(2 + KC)]
        ld_ahead = [sem(f"ld_ahead{u}") for u in range(AHEAD)]
        ld_wout, ld_w2, ld_bdn, ld_bgu = sem("ld_wout"), sem("ld_w2"), sem("ld_bdn"), sem("ld_bgu")
        ld_down_ahead = sem("ld_down_ahead")
        landed = [sem(f"landed{c}") for c in range(RING)]
        split = sem("split")
        stored = sem("stored")
        dv = sem("dv")
        x_ss = sem("x_ss")
        xT_psum, xT_sb, proj = sem("xT_psum"), sem("xT_sb"), sem("proj")
        weighed = sem("weighed")
        rstd1, rstd2 = sem("rstd1"), sem("rstd2")
        trig_arg, trig_done = sem("trig_arg"), sem("trig_done")
        qk_out, uv_out, roped = sem("qk_out"), sem("uv_out"), sem("roped")
        qkT_psum, qkT_sb = sem("qkT_psum"), sem("qkT_sb")
        scores, maxed, exped, probs = sem("scores"), sem("maxed"), sem("exped"), sem("probs")
        PT_psum, PT_a, PT_v = sem("PT_psum"), sem("PT_a"), sem("PT_v")
        oT_psum, oT_sb = sem("oT_psum"), sem("oT_sb")
        pooled_psum, pooled_sb, mix_psum, mix_sb = sem("pooled_psum"), sem("pooled_sb"), sem("mix_psum"), sem("mix_sb")
        pool_used, half_used = sem("pool_used"), sem("half_used")
        h_psum, h_sb, h_ss, n2_sb = sem("h_psum"), sem("h_sb"), sem("h_ss"), sem("n2_sb")
        opened, order_ready = sem("opened"), sem("order_ready")
        hT_psum, hT_a, hT_v, logits = sem("hT_psum"), sem("hT_a"), sem("hT_v"), sem("logits")
        top_in, top_exp, gates = sem("top_in"), sem("top_exp"), sem("gates")
        picked, wr_ready = sem("picked"), sem("wr_ready")
        ranks, GdT_psum, GdT_sb, count_ready = sem("ranks"), sem("GdT_psum"), sem("GdT_sb"), sem("count_ready")
        pieces_used = sem("pieces_used")
        s_ready, sg_ready, oneh_ready = sem("s_ready"), sem("sg_ready"), sem("oneh_ready")
        gathered, xe_sb = sem("gathered"), sem("xe_sb")
        gu_done, g_ready, sig_ready, act_ready = sem("gu_done"), sem("g_ready"), sem("sig_ready"), sem("act_ready")
        u_ready, ug_ready = sem("u_ready"), sem("ug_ready")
        aT_psum, aT_sb = sem("aT_psum"), sem("aT_sb")
        gt_psum, gt_sb, y_sb = sem("gt_psum"), sem("gt_sb"), sem("y_sb")
        acc_final, out_a, out_v = sem("acc_final"), sem("out_a"), sem("out_v")

        block = ctx.enter_context(nc.Block())

        def more_passes(eng, count, body, after=None):
            eng.wait_ge(count_ready, 1)
            most = eng.value_load(cnti[0:1, 0:1].bitcast(I32), min_val=0, max_val=SEQ)
            with eng.If(most > SLOTS):
                with eng.Fori(1, PASSES) as p:
                    with eng.Fori(0, count) as e:
                        body(p, e)
                if after:
                    after()

        @block.sync
        def _(sp):
            for t in range(T):
                sp.dma_start(X[:, t, :], x_t[:, t, :]).then_inc(ld_x[t], 16)
            for k in range(KC):
                sp.dma_start(win[:, k, 0:QKW + VW], w_in_k[:, k, 0:QKW + VW]).then_inc(ld_win[k], 16)
            for k in range(0, KC, 4):
                sp.dma_start(win[:, k:k + 4, QKW + VW:INW], w_in_k[:, k:k + 4, QKW + VW:INW]).then_inc(ld_winu, 16)
            sp.dma_start(band, bands.rearrange("p (g s) -> p g s", g=NG)).then_inc(ld_bands, 16)
            sp.dma_start(poolw, pool_w.rearrange("g c d -> c g d")).then_inc(ld_bands, 16)
            sp.dma_start(wout[:, 0:NG, :], w_out_p).then_inc(ld_wout, 16)
            for g in range(NKV):
                sp.dma_start(wout[g * HD:(g + 1) * HD, NG:KC, :], w_out_a[g]).then_inc(ld_wout, 16)

            def load_piece(s, first=0, skip=0, stop=4):
                slot, e, c = s % RING, first + s // PIECES, s % PIECES
                if c < GU_PIECES:
                    chunks, row, src = 2, 2 * c, w_gu_k
                else:
                    chunks, row, src = 4, 4 * (c - GU_PIECES), w_dn_k
                dst = ring[:, slot * PIECE:(slot + 1) * PIECE].rearrange("p (k n) -> p k n", k=chunks)
                n = min(chunks, stop) - skip
                sp.dma_start(dst[:, skip:skip + n, :], src[:, bass.ds(e * KC + row + skip, n), :]).then_inc(landed[slot], 16)

            def load_ahead(n):
                src = w_gu_k[:, (NE - 2 * TURN + n // 2) * KC, :].rearrange("p (f j n) -> p j f n", f=2, j=2)
                sp.dma_start(ahead[n], src[:, n % 2]).then_inc(ld_ahead[n // 2], 16)

            for s in range(3):
                load_piece(s)
            sp.wait_ge(proj, 4)
            for s in range(3, 5):
                load_piece(s)
            load_ahead(0)
            sp.wait_ge(mix_psum, 1)
            load_piece(5)
            sp.dma_start(w2b, norm2_w.rearrange("(a n) -> a n", a=1).to_broadcast([P, DM])).then_inc(ld_w2, 16)
            sp.wait_ge(scores, ROUNDS)
            load_ahead(1)
            sp.wait_ge(pool_used, 1)
            load_piece(6)
            sp.dma_start(down_ahead, w_dn_k[:, (NE - 2 * TURN) * KC, :]).then_inc(ld_down_ahead, 16)
            sp.wait_ge(PT_psum, 2)
            load_ahead(2)
            sp.wait_ge(half_used, 1)
            load_piece(7, stop=1)
            sp.wait_ge(h_psum, 2 * T)
            load_piece(7, skip=1)
            load_ahead(3)
            load_ahead(4)
            sp.wait_ge(opened, 1)
            sp.wait_ge(h_ss, 1)
            sp.wait_ge(n2_sb, 1)
            load_ahead(5)
            sp.wait_ge(n2_sb, T)
            load_ahead(6)
            sp.wait_ge(opened, T)
            load_ahead(7)
            sp.wait_ge(sg_ready, 1)
            load_ahead(8)
            load_ahead(9)

            with sp.Fori(0, TURNS - 3) as r:
                for s in range(TP):
                    sp.wait_ge(pieces_used, r * TP + s + 1)
                    load_piece(RING + s, r * TURN)
            for s in range(RING, 3 * TP):
                sp.wait_ge(pieces_used, (TURNS - 3) * TP + s - RING + 1)
                if s == TP + RING:
                    sp.dma_start(bdn, b_down).then_inc(ld_bdn, 16)
                if s < 3 * TP - 3:
                    gu_ahead = 0 <= s - TP < AHEAD * PIECES and s % PIECES == 0
                    load_piece(s, NE - 3 * TURN, skip=1 if gu_ahead or s == TP + GU_PIECES else 0)
                    continue
                if s == 3 * TP - 3:
                    chunks, row, src, first = 2, KC - 2, w_gu_k, 0
                else:
                    row = 4 * (s - (3 * TP - 2))
                    chunks, src, first = 4, w_dn_k, 2 + row
                dst = ring[:, s % RING * PIECE:(s % RING + 1) * PIECE].rearrange("p (k n) -> p k n", k=chunks)
                for k in range(chunks):
                    sp.dma_start(dst[:, k, :], src[:, (NE - 1) * KC + row + k, :]).then_inc(landed_last[first + k], 16)

            def next_pass(p, r):
                for s in range(TP):
                    sp.wait_ge(pieces_used, p * (NE * PIECES) + r * TP + (s + 1 - RING))
                    load_piece(s, r * TURN)

            more_passes(sp, TURNS, next_pass)

            for t in range(T):
                for c, done in enumerate((out_v, out_a)):
                    sp.wait_ge(done, t + 1)
                    sp.dma_start(out_t[t][:, 512 * c:512 * c + 512], X[:, t, 512 * c:512 * c + 512]).then_inc(stored, 16)
            sp.wait_ge(stored, 16 * T * 2)

        @block.gpsimd
        def _(pool):
            pool.wait_ge(ld_small, 16 * 8)
            nc.gpsimd.tensor_copy(tri[:, :], tri32).then_inc(order_ready, 1)
            pool.wait_ge(ld_late, 32)
            nc.gpsimd.tensor_copy(ones[:, :], C[:, C_ONE:C_ONE + P]).then_inc(order_ready, 1)
            f = N2[0:3 * NE, :, :].rearrange("p t n -> p (t n)")
            pool.wait_ge(ld_bgu, 48)
            nc.gpsimd.tensor_copy(bgs[:, :], f).then_inc(split, 1)
            for n in range(1, 3):
                rows = slice(0, (3 - n) * NE)
                pool.wait_ge(split, 2 * n - 1)
                nc.gpsimd.tensor_tensor(f[rows], f[rows], bgs[rows, :], ALU.subtract).then_inc(split, 1)
                pool.wait_ge(split, 2 * n)
                nc.gpsimd.tensor_copy(bgs[rows, :], f[rows]).then_inc(split, 1)
            pool.wait_ge(split, 5)
            pool.wait_ge(ld_w2, 16)
            pool.wait_ge(h_sb, 2 * T)
            nc.gpsimd.tensor_tensor(N2[:, 1, :], X[:, 1, :], w2b, ALU.mult).then_inc(weighed, 1)

        @block.scalar
        def _(act):
            act.dma_start(ident, consts[:, C_ID:C_ID + P]).then_inc(ld_id, 16)
            act.dma_start(w1c, norm1_w.rearrange("(k p) -> p k", p=P), allow_slow_non_contiguous=True).then_inc(ld_c, 16)
            act.dma_start(posi.bitcast(I32), positions.rearrange("b (t p) -> p (b t)", p=P), allow_slow_non_contiguous=True).then_inc(ld_small, 16)
            act.dma_start(scl, pool_scale.rearrange("(g p) -> p g", p=P), allow_slow_non_contiguous=True).then_inc(ld_small, 16)
            act.dma_start(w2c, norm2_w.rearrange("(k p) -> p k", p=P), allow_slow_non_contiguous=True).then_inc(ld_small, 16)
            for dst, src in ((qnw, q_norm_w), (knw, k_norm_w), (sink, sinks), (brt, b_router)):
                row = src.rearrange("(a n) -> a n", a=1)
                act.dma_start(dst, row.to_broadcast([P, row.shape[1]])).then_inc(ld_small, 16)
            act.dma_start(passing[:, 0:NC_COLS - C_FRONT], consts[:, C_FRONT:NC_COLS]).then_inc(ld_small, 16)
            act.dma_start(C[:, C_ONE:C_FRONT], consts[:, C_ONE:C_FRONT]).then_inc(ld_late, 16)
            act.dma_start(wr, w_router.rearrange("(k p) e -> p k e", p=P)).then_inc(ld_late, 16)
            for n in range(3):
                act.dma_start(N2[n * NE:(n + 1) * NE, :, :].rearrange("p t n -> p (t n)"), b_gu).then_inc(ld_bgu, 16)

            for t in range(T):
                act.wait_ge(ld_x[t], 16)
                nc.scalar.activation(PR[:, t, :], X[:, t, :], ACT.Square, accum_out=nrm[:, t:t + 1]).then_inc(x_ss, 1)
            act.wait_ge(trig_arg, 1)
            nc.scalar.activation(trig, turn, ACT.Sin).then_inc(trig_done, 1)

            def proj_out(t, src, dst, s):
                nc.scalar.activation(dst, src, ACT.Copy, scale=rms[:, t:t + 1]).then_inc(s, 1)

            def qkv_out(t):
                act.wait_ge(proj, t + 1)
                for g in range(NKV):
                    proj_out(t, ps[:, Q_BANK[t], g * GRP * HD:(g + 1) * GRP * HD].rearrange("p (h d) -> p h d", h=GRP),
                             qk[:, t, 0:ATT].rearrange("p (h g d) -> p g h d", g=NKV, h=GRP)[:, g], qk_out)
                proj_out(t, ps[:, KV_BANK[t], 0:VW], qk[:, t, ATT:QKW], qk_out)
                proj_out(t, ps[:, KV_BANK[t], VW:2 * VW], V[:, t, :], uv_out)

            def u_out(t):
                act.wait_ge(proj, 2 + t + 1)
                proj_out(t, ps[:, U_BANK[t], :], U[:, t, :], uv_out)

            def qkT_out(t):
                act.wait_ge(qkT_psum, t + 1)
                nc.scalar.copy(qT[:, :, t * P:(t + 1) * P], ps[:, 6, :].rearrange("p (h s) -> p h s", h=GRP)).then_inc(qkT_sb, 1)
                nc.scalar.copy(kT[:, t * P:(t + 1) * P], ps[:, 7, 0:P]).then_inc(qkT_sb, 1)

            def softmax_exp(r):
                heads = NQ if r == 0 else NQ // 2
                keys = 1024 // heads
                act.wait_ge(maxed, r + 1)
                for j in range(heads):
                    pr = PR[:, r % 2, j * keys:(j + 1) * keys]
                    nc.scalar.activation(pr, pr, ACT.Exp, bias=nm[:, j:j + 1], accum_out=sm[:, j:j + 1]).then_inc(exped, 1)
                nc.scalar.activation(es[:, 0:heads], es[:, 0:heads], ACT.Exp).then_inc(exped, 1)

            def pt_out(r):
                act.wait_ge(PT_psum, r + 1)
                nc.scalar.copy(PT[:, r % 2, 0:512], ps[:, SET[r][0], :]).then_inc(PT_a, 1)

            act.wait_ge(rstd1, 1)
            qkv_out(0)
            qkv_out(1)
            qkT_out(0)
            u_out(0)
            softmax_exp(0)
            u_out(1)
            qkT_out(1)
            for b, bank in enumerate(POOLED):
                act.wait_ge(pooled_psum, 1)
                nc.scalar.copy(pooled[:, 2 * b:2 * b + 2, :], ps[:, bank, :].rearrange("p (g s) -> p g s", g=2)).then_inc(pooled_sb, 1)
            pt_out(0)
            act.wait_ge(mix_psum, 1)
            for g in range(NG):
                nc.scalar.activation(mixP[:, g, :], ps[:, MIXED[g // 2], 256 * (g % 2):256 * (g % 2) + 256], ACT.Copy,
                                     scale=scl[:, g:g + 1]).then_inc(mix_sb, 1)
            softmax_exp(1)
            pt_out(1)
            softmax_exp(2)
            pt_out(2)

            for t in range(T):
                act.wait_ge(h_sb, 2 * t + 2)
                nc.scalar.activation(squares, X[:, t, :], ACT.Square, accum_out=nrm[:, t:t + 1]).then_inc(h_ss, 1)
                act.wait_ge(hT_psum, 2 * t + 1)
                nc.scalar.copy(tT[:, 0:4, t * P:(t + 1) * P], ps[:, ACC[t], :].rearrange("p (k s) -> p k s", k=4)).then_inc(hT_a, 1)
                if t == 1:
                    act.wait_ge(weighed, 1)
                    act.wait_ge(rstd2, T)
                    nc.scalar.activation(N2[:, 1, :], N2[:, 1, :], ACT.Copy, scale=rms[:, 1:2]).then_inc(n2_sb, 1)
                act.wait_ge(top_in, t + 1)
                nc.scalar.activation(gts[:, t, 0:TOPK], top[:, t, 0:TOPK], ACT.Exp, bias=lm[:, t:t + 1],
                                     accum_out=gsum[:, t, 0:1]).then_inc(top_exp, 1)
            act.wait_ge(gathered, 1)
            nc.scalar.copy(xe, ps[:, GAT, :].rearrange("p (k s) -> p k s", k=KC)).then_inc(xe_sb, 1)
            act.wait_ge(GdT_psum, 1)
            nc.scalar.copy(GdT, ps[0:NE, DWN, 0:T * P].rearrange("p (t s) -> p t s", t=T)).then_inc(GdT_sb, 1)

            def expert(n):
                for b in range(2):
                    act.wait_ge(g_ready, 2 * n + b + 1)
                    nc.scalar.activation(sg[:, b, :], gb[:, b, :], ACT.Sigmoid, scale=ALPHA).then_inc(sig_ready, 1)
                act.wait_ge(gathered, n + 2)
                nc.scalar.copy(xe, ps[:, GAT, :].rearrange("p (k s) -> p k s", k=KC)).then_inc(xe_sb, 1)
                act.wait_ge(gt_psum, n + 1)
                nc.scalar.copy(GT, ps[:, GAT, 0:T * P].rearrange("p (t s) -> p t s", t=T)).then_inc(gt_sb, 1)
                act.wait_ge(pieces_used, n * PIECES + PIECES)
                nc.scalar.copy(ye, ps[:, DWN, :]).then_inc(y_sb, 1)

            with act.Fori(0, NE) as e:
                expert(e)
            more_passes(act, NE, lambda p, e: expert(p * NE + e))

            for t in range(T):
                act.wait_ge(acc_final, 2 * t + 2)
                nc.scalar.copy(X[:, t, 512:1024], ps[:, ACC[t] + 1, :]).then_inc(out_a, 1)

        @block.vector
        def _(dve):
            steps = [0]

            def link(ins):
                steps[0] += 1
                ins.then_inc(dv, 1)
                dve.wait_ge(dv, steps[0])

            def rsqrt(y, v, t):
                link(nc.vector.tensor_scalar(y.bitcast(I32), v.bitcast(I32), 1, None, ALU.logical_shift_right))
                link(nc.vector.tensor_scalar(y.bitcast(I32), y.bitcast(I32), -1.0, RSQRT_MAGIC, ALU.mult, ALU.add))
                for n in range(3):
                    link(nc.vector.tensor_tensor(t, y, y, ALU.mult))
                    link(nc.vector.scalar_tensor_tensor(t, t, -0.5, v, ALU.mult, ALU.mult))
                    last = nc.vector.scalar_tensor_tensor(y, t, 1.5, y, ALU.add, ALU.mult)
                    if n < 2:
                        link(last)
                return last

            dve.wait_ge(ld_c, 16)
            for n in range(2 * T):
                t, b = n // 2, n % 2
                dve.wait_ge(xT_psum, n + 1)
                nc.vector.tensor_tensor(tT[:, 4 * b:4 * b + 4, t * P:(t + 1) * P],
                                        ps[:, 6 + b, :].rearrange("p (k s) -> p k s", k=4),
                                        w1c[:, 4 * b:4 * b + 4].unsqueeze(2).to_broadcast([P, 4, P]),
                                        ALU.mult).then_inc(xT_sb, 1)
            dve.wait_ge(x_ss, T)
            link(nc.vector.tensor_scalar(nrm, nrm, 1.0 / DM, EPS, ALU.mult, ALU.add))
            rsqrt(rms, nrm, rt[:, 0:T]).then_inc(rstd1, 1)

            dve.wait_ge(ld_small, 16 * 8)
            link(nc.vector.tensor_copy(posf, posi.bitcast(I32)))
            for t in range(T):
                for f in range(2):
                    link(nc.vector.tensor_scalar(trig[:, t, f, :], freq, posf[:, t:t + 1], None, ALU.mult))
            for f in range(2):
                link(nc.vector.tensor_scalar(turn[:, :, f, :], trig[:, :, f, :], TWO_PI_INV, 0.25 * f, ALU.mult, ALU.add))
            link(nc.vector.tensor_scalar(turn, turn, ROUND, None, ALU.add))
            link(nc.vector.tensor_scalar(turn, turn, ROUND, None, ALU.subtract))
            tf, af = (v.rearrange("p t f h -> p (t f h)") for v in (turn, trig))
            for part in (PI_A, PI_B, PI_C):
                link(nc.vector.scalar_tensor_tensor(af, tf, -part, af, ALU.mult, ALU.add))
            for f in range(2):
                link(nc.vector.tensor_scalar(trig[:, :, f, :], trig[:, :, f, :], f * float(np.pi / 2), SIN_MAX, ALU.add, ALU.min))
            nc.vector.tensor_scalar(tf, af, -SIN_MAX, None, ALU.max).then_inc(trig_arg, 1)

            def norm_rope(t):
                heads = qk[:, t, :].rearrange("p (h d) -> p h d", d=HD)
                sq = tmp[:, 0:QKW].rearrange("p (h d) -> p h d", d=HD)
                dve.wait_ge(qk_out, 3 * t + 3)
                link(nc.vector.tensor_tensor(sq, heads, heads, ALU.mult))
                link(nc.vector.tensor_reduce(ss, sq, AX_X, ALU.add))
                link(nc.vector.tensor_scalar(ss, ss, 1.0 / HD, QK_EPS, ALU.mult, ALU.add))
                link(rsqrt(rs, ss, rt))
                link(nc.vector.tensor_tensor(heads, heads, rs.unsqueeze(2).to_broadcast([P, NH, HD]), ALU.mult))
                for w, a, b in ((qnw, 0, NQ), (knw, NQ, NH)):
                    link(nc.vector.tensor_tensor(heads[:, a:b, :], heads[:, a:b, :], w.unsqueeze(1).to_broadcast([P, b - a, HD]), ALU.mult))
                pair = heads[:, :, 0:2 * HALF].rearrange("p h (f d) -> p h f d", f=2)
                by_cos = tmp[:, 640:640 + 16 * NH].rearrange("p (h f d) -> p h f d", h=NH, f=2)
                by_sin = tmp[:, 800:800 + 16 * NH].rearrange("p (h f d) -> p h f d", h=NH, f=2)
                if t == 0:
                    dve.wait_ge(trig_done, 1)
                for f, dst in ((1, by_cos), (0, by_sin)):
                    table = trig[:, t, f, :].unsqueeze(1).unsqueeze(1).to_broadcast([P, NH, 2, HALF])
                    link(nc.vector.tensor_tensor(dst, pair, table, ALU.mult))
                nc.vector.tensor_tensor(pair[:, :, 0, :], by_cos[:, :, 0, :], by_sin[:, :, 1, :], ALU.subtract)
                nc.vector.tensor_tensor(pair[:, :, 1, :], by_cos[:, :, 1, :], by_sin[:, :, 0, :], ALU.add).then_inc(roped, 1)
                dve.wait_ge(roped, t + 1)

            def softmax_in(r):
                heads = NQ if r == 0 else NQ // 2
                keys = 1024 // heads
                half = heads // 2
                dve.wait_ge(scores, r + 1)
                allowed = mask[:, 2 * P - keys:2 * P].unsqueeze(1).to_broadcast([P, half, keys])
                for g in range(NKV):
                    link(nc.vector.scalar_tensor_tensor(
                        PR[:, r % 2, 512 * g:512 * g + 512].rearrange("p (h k) -> p h k", h=half),
                        ps[:, SET[r][g], :].rearrange("p (h k) -> p h k", h=half),
                        HD ** -0.5, allowed, ALU.mult, ALU.add))
                link(nc.vector.tensor_reduce(mx[:, 0:heads], PR[:, r % 2, :].rearrange("p (h k) -> p h k", h=heads), AX_X, ALU.max))
                first = 0 if r < 2 else 2
                sk = sink.rearrange("p (g h) -> p g h", g=NKV)[:, :, first:first + half]
                mg, eg = (v[:, 0:heads].rearrange("p (g h) -> p g h", g=NKV) for v in (mx, es))
                link(nc.vector.tensor_tensor(mg, mg, sk, ALU.max))
                link(nc.vector.tensor_tensor(eg, sk, mg, ALU.subtract))
                nc.vector.tensor_scalar(nm[:, 0:heads], mx[:, 0:heads], -1.0, None, ALU.mult).then_inc(maxed, 1)

            def softmax_out(r):
                heads = NQ if r == 0 else NQ // 2
                keys = 1024 // heads
                dve.wait_ge(exped, (0, 9, 14)[r] + heads + 1)
                link(nc.vector.tensor_tensor(sm[:, 0:heads], sm[:, 0:heads], es[:, 0:heads], ALU.add))
                link(nc.vector.reciprocal(rc[:, 0:heads], sm[:, 0:heads]))
                pr = PR[:, r % 2, :].rearrange("p (h k) -> p h k", h=heads)
                nc.vector.tensor_tensor(pr, pr, rc[:, 0:heads].unsqueeze(2).to_broadcast([P, heads, keys]), ALU.mult).then_inc(probs, 1)

            def pt_out(r):
                dve.wait_ge(PT_psum, r + 1)
                if r == 1:
                    dve.wait_ge(mix_psum, 1)
                nc.vector.tensor_copy(PT[:, r % 2, 512:1024], ps[:, SET[r][1], :]).then_inc(PT_v, 1)

            def ot_out(r):
                dve.wait_ge(oT_psum, r + 1)
                a, n, s = ((0, GRP, 0), (0, 2, P), (2, 2, P))[r]
                nc.vector.tensor_copy(mixA[:, a:a + n, s:s + P],
                                      ps[:, SET[r][0], 0:n * P].rearrange("p (h s) -> p h s", h=n)).then_inc(oT_sb, 1)

            def h_out(t):
                for c in range(2):
                    dve.wait_ge(h_psum, 2 * t + c + 1)
                    half = X[:, t, 512 * c:512 * c + 512]
                    nc.vector.tensor_tensor(half, half, ps[:, ACC[t] + c, :], ALU.add).then_inc(h_sb, 1)

            def rms2(t):
                dve.wait_ge(h_ss, t + 1)
                link(nc.vector.tensor_scalar(nrm[:, t:t + 1], nrm[:, t:t + 1], 1.0 / DM, EPS, ALU.mult, ALU.add))
                rsqrt(rms[:, t:t + 1], nrm[:, t:t + 1], rt[:, t:t + 1]).then_inc(rstd2, 1)
                dve.wait_ge(rstd2, t + 1)

            def hT_out(t):
                dve.wait_ge(hT_psum, 2 * t + 2)
                nc.vector.tensor_copy(tT[:, 4:8, t * P:(t + 1) * P],
                                      ps[:, ACC[t] + 1, :].rearrange("p (k s) -> p k s", k=4)).then_inc(hT_v, 1)

            def pick(t):
                dve.wait_ge(logits, t + 1)
                link(nc.vector.scalar_tensor_tensor(lg[:, t, :], ps[:, LOGITS, t * NE:(t + 1) * NE], rms[:, t:t + 1], brt, ALU.mult, ALU.add))
                link(nc.vector.max(top[:, t, :], lg[:, t, :]))
                nc.vector.tensor_scalar(lm[:, t:t + 1], top[:, t, 0:1], -1.0, None, ALU.mult).then_inc(top_in, 1)
                link(nc.vector.max_index(topi[:, t, :].bitcast(U32), top[:, t, :], lg[:, t, :]))
                link(nc.vector.tensor_tensor(hot[:, t], iota[:, 0:NE].unsqueeze(1).to_broadcast([P, TOPK, NE]),
                                             topi[:, t, 0:TOPK].bitcast(U32).unsqueeze(2).to_broadcast([P, TOPK, NE]), ALU.is_equal))
                with nc.allow_low_precision(reason="at most one of a token's four is an expert: the sum is 0 or 1"):
                    nc.vector.tensor_reduce(sel[:, t, :], hot[:, t].rearrange("p j e -> p e j"), AX_X, ALU.add).then_inc(picked, 1)

            def weigh(t):
                dve.wait_ge(top_exp, t + 1)
                link(nc.vector.reciprocal(gsum[:, t, 1:2], gsum[:, t, 0:1]))
                link(nc.vector.tensor_scalar(gts[:, t, 0:TOPK], gts[:, t, 0:TOPK], gsum[:, t, 1:2], None, ALU.mult))
                link(nc.vector.tensor_tensor(hotg[:, t], hot[:, t], gts[:, t, 0:TOPK].unsqueeze(2).to_broadcast([P, TOPK, NE]), ALU.mult))
                nc.vector.tensor_reduce(Gd[:, t, :], hotg[:, t].rearrange("p j e -> p e j"), AX_X, ALU.add).then_inc(gates, 1)

            norm_rope(0)
            norm_rope(1)
            softmax_in(0)
            softmax_out(0)
            pt_out(0)
            softmax_in(1)
            ot_out(0)
            softmax_out(1)
            softmax_in(2)
            dve.wait_ge(ld_late, 32)
            nc.vector.tensor_tensor(wr, wr, w2c.unsqueeze(2).to_broadcast([P, KC, NE]), ALU.mult).then_inc(wr_ready, 1)
            pt_out(1)
            softmax_out(2)
            ot_out(1)
            pt_out(2)
            h_out(0)
            ot_out(2)
            hT_out(0)
            rms2(0)
            dve.wait_ge(ld_w2, 16)
            dve.wait_ge(split, 5)
            nc.vector.scalar_tensor_tensor(N2[:, 0, :], X[:, 0, :], rms[:, 0:1], w2b, ALU.mult, ALU.mult).then_inc(n2_sb, 1)
            pick(0)
            weigh(0)
            h_out(1)
            hT_out(1)
            rms2(1)
            pick(1)
            dve.wait_ge(ranks, 1)
            link(nc.vector.scalar_tensor_tensor(rk, ps[:, RANKS, 0:T * NE].rearrange("p (t e) -> p t e", t=T), 1.0, sel[:, :, :], ALU.add, ALU.mult))
            link(nc.vector.tensor_tensor(rank.rearrange("p t (r e) -> p t r e", e=NE),
                                         rk.unsqueeze(2).to_broadcast([P, T, PASSES + 1, NE]),
                                         passed.rearrange("p (r e) -> p r e", e=NE).unsqueeze(1).to_broadcast([P, T, PASSES + 1, NE]),
                                         ALU.add))

            def build_s(n):
                for t in range(T):
                    ins = nc.vector.tensor_scalar(S1[:, t, :], iota[:, 0:SLOTS], rank[:, t, bass.ds(n, 1)], None, ALU.is_equal)
                ins.then_inc(s_ready, 1)

            def build_sg(n):
                for t in range(T):
                    ins = nc.vector.tensor_scalar(SG[:, t, :], iota, rank[:, t, bass.ds(n, 1)], gate[:, t, bass.ds(n, 1)], ALU.is_equal, ALU.mult)
                ins.then_inc(sg_ready, 1)

            def build_oneh(e):
                nc.vector.tensor_scalar(oneh[:, :], C[0:3 * NE, C_ONE:C_ONE + SLOTS], C[0:3 * NE, bass.ds(e + C_EXP, 1)], None, ALU.mult).then_inc(oneh_ready, 1)

            build_s(0)
            build_oneh(0)
            link(nc.vector.tensor_reduce(cnt, ps[:, RANKS, T * NE:(T + 1) * NE], AX_X, ALU.max))
            nc.vector.tensor_copy(cnti.bitcast(I32), cnt).then_inc(count_ready, 1)
            weigh(1)
            dve.wait_ge(gates, T)
            link(nc.vector.tensor_copy(gate.rearrange("p t (r e) -> p t r e", e=NE), Gd.unsqueeze(2).to_broadcast([P, T, PASSES + 1, NE])))
            build_sg(0)
            gu = ps[:, GU:GU + 2, :].rearrange("p b (f n) -> p b f n", f=2)

            def expert(n, e):
                dve.wait_ge(gathered, n + 1)
                build_s(n + 1)
                for b in range(2):
                    dve.wait_ge(gu_done, 2 * n + b + 1)
                    nc.vector.tensor_scalar(gb[:, b, :], gu[:, b, 0, :], LIMIT, None, ALU.min).then_inc(g_ready, 1)
                    nc.vector.tensor_scalar(ub[:, b, :], gu[:, b, 1, :], LIMIT, -LIMIT, ALU.min, ALU.max).then_inc(u_ready, 1)
                for b in range(2):
                    dve.wait_ge(u_ready, 2 * n + b + 1)
                    dve.wait_ge(g_ready, 2 * n + b + 1)
                    nc.vector.scalar_tensor_tensor(ub[:, b, :], ub[:, b, :], 1.0, gb[:, b, :], ALU.add, ALU.mult).then_inc(ug_ready, 1)
                for b in range(2):
                    dve.wait_ge(ug_ready, 2 * n + b + 1)
                    dve.wait_ge(sig_ready, 2 * n + b + 1)
                    nc.vector.tensor_tensor(ab[:, b, :], ub[:, b, :], sg[:, b, :], ALU.mult).then_inc(act_ready, 1)
                build_oneh((e + 1) % NE)
                dve.wait_ge(aT_psum, 2 * n + 2)
                nc.vector.tensor_copy(aT, ps[:, DWN, :].rearrange("p (f s) -> p f s", f=4)).then_inc(aT_sb, 1)
                dve.wait_ge(gt_psum, n + 1)
                build_sg(n + 1)

            with dve.Fori(0, NE) as e:
                expert(e, e)
            more_passes(dve, NE, lambda p, e: expert(p * NE + e, e))

            for t in range(T):
                dve.wait_ge(acc_final, 2 * t + 2)
                nc.vector.tensor_copy(X[:, t, 0:512], ps[:, ACC[t], :]).then_inc(out_v, 1)

        @block.tensor
        def _(pe):
            mm = nc.tensor.matmul
            pe.wait_ge(ld_id, 16)
            for n in range(2 * T):
                t, b = n // 2, n % 2
                if b == 0:
                    pe.wait_ge(ld_x[t], 16)
                if n >= 2:
                    pe.wait_ge(xT_sb, n - 1)
                for k in range(4):
                    kc = 4 * b + k
                    last = nc.tensor.transpose(ps[:, 6 + b, k * P:(k + 1) * P], X[:, t, kc * P:(kc + 1) * P], ident)
                last.then_inc(xT_psum, 1)

            def project(t, parts, chunks=range(KC)):
                for k in chunks:
                    if parts[0][1] == 0:
                        pe.wait_ge(ld_win[k], 16)
                    elif k % 4 == 0:
                        pe.wait_ge(ld_winu, 32)
                    for bank, a, w in parts:
                        last = mm(ps[:, bank, 0:w], tT[:, k, t * P:(t + 1) * P], win[:, k, a:a + w], start=k == 0, stop=k == KC - 1)
                if k == KC - 1:
                    last.then_inc(proj, 1)

            def qkv(t):
                return [(Q_BANK[t], 0, ATT), (KV_BANK[t], ATT, 2 * VW)]

            def pool_in(t):
                return [(U_BANK[t], QKW + VW, PW)]

            pe.wait_ge(xT_sb, 2)
            project(0, qkv(0))
            pe.wait_ge(xT_sb, 4)
            project(1, qkv(1))
            project(0, pool_in(0))

            def transpose_qk(t):
                for h in range(GRP):
                    nc.tensor.transpose(ps[:, 6, h * P:(h + 1) * P], qk[:, t, h * P:(h + 1) * P], ident)
                nc.tensor.transpose(ps[:, 7, 0:P], qk[:, t, ATT:QKW], ident).then_inc(qkT_psum, 1)

            def score(r):
                t = 0 if r == 0 else 1
                keys = P if r == 0 else SEQ
                heads = range(GRP) if r == 0 else range(2 * r - 2, 2 * r)
                for n, h in enumerate(heads):
                    for g in range(NKV):
                        rows = slice(g * HD, (g + 1) * HD)
                        last = mm(ps[:, SET[r][g], n * keys:(n + 1) * keys], qT[rows, h, t * P:(t + 1) * P], kT[rows, 0:keys],
                                  start=True, stop=True)
                last.then_inc(scores, 1)

            def transpose_probs(r):
                pe.wait_ge(probs, r + 1)
                for j in range(8):
                    last = nc.tensor.transpose(ps[:, SET[r][j // 4], (j % 4) * P:(j % 4 + 1) * P], PR[:, r % 2, j * P:(j + 1) * P], ident)
                last.then_inc(PT_psum, 1)

            def attend(r):
                pe.wait_ge(PT_a, r + 1)
                pe.wait_ge(PT_v, r + 1)
                blocks = 1 if r == 0 else 2
                n = 4 // blocks
                for kb in range(blocks):
                    for g in range(NKV):
                        pt = PT[:, r % 2, 512 * g:512 * g + 512].rearrange("p (h k q) -> p h k q", h=n, k=blocks)
                        last = mm(ps[g * HD:(g + 1) * HD, SET[r][0], 0:n * P].rearrange("p (h q) -> p h q", h=n), V[:, kb, g * HD:(g + 1) * HD], pt[:, :, kb, :],
                                  start=kb == 0, stop=kb == blocks - 1)
                last.then_inc(oT_psum, 1)

            def out_project(t, src, first, heads, banks=range(2)):
                for h in heads:
                    for c in banks:
                        last = mm(ps[:, ACC[t] + c, :], src[:, h, t * P:(t + 1) * P], wout[:, first + h, 512 * c:512 * c + 512],
                                  start=first == 0 and h == 0, stop=first == NG and h == GRP - 1)
                return last

            pe.wait_ge(roped, 1)
            transpose_qk(0)
            pe.wait_ge(qk_out, 6)
            pe.wait_ge(uv_out, 2)
            project(1, pool_in(1), range(1))
            pe.wait_ge(qkT_sb, 2)
            score(0)
            project(1, pool_in(1), range(1, KC))
            pe.wait_ge(roped, 2)
            transpose_qk(1)
            pe.wait_ge(ld_bands, 32)
            pe.wait_ge(uv_out, 3)
            for g in range(NG):
                o = ps[:, POOLED[g // 2], 256 * (g % 2):256 * (g % 2) + SEQ]
                mm(o[:, 0:P], U[:, 0, g * P:(g + 1) * P], band[:, g, 0:P], start=True, stop=True)
                mm(o[:, P:SEQ], U[:, 0, g * P:(g + 1) * P], band[:, g, P:SEQ], start=True, stop=False)
                pe.wait_ge(uv_out, 4)
                last = mm(o[:, P:SEQ], U[:, 1, g * P:(g + 1) * P], band[:, g, SEQ:SEQ + P], start=False, stop=True)
            last.then_inc(pooled_psum, 1)
            pe.wait_ge(qkT_sb, 4)
            score(1)
            transpose_probs(0)
            for g in range(NG):
                if g % 2 == 0:
                    pe.wait_ge(pooled_sb, g // 2 + 1)
                last = mm(ps[:, MIXED[g // 2], 256 * (g % 2):256 * (g % 2) + SEQ], poolw[:, g, :], pooled[:, g, :], start=True, stop=True)
            last.then_inc(mix_psum, 1)
            attend(0)
            pe.wait_ge(ld_wout, 48)
            for g in range(NG):
                pe.wait_ge(mix_sb, max(g + 1, 2))
                out_project(0, mixP, 0, [g])
            pe.wait_ge(oT_sb, 1)
            score(2)
            transpose_probs(1)
            out_project(1, mixP, 0, range(4)).then_inc(pool_used, 1)
            attend(1)
            transpose_probs(2)
            for c in range(2):
                out_project(0, mixA, NG, range(4), [c]).then_inc(h_psum, 1)
            attend(2)

            def transpose_h(t):
                for b in range(2):
                    pe.wait_ge(h_sb, 2 * t + b + 1)
                    for k in range(4):
                        last = nc.tensor.transpose(ps[:, ACC[t] + b, k * P:(k + 1) * P], X[:, t, (4 * b + k) * P:(4 * b + k + 1) * P], ident)
                    last.then_inc(hT_psum, 1)

            def route(t):
                pe.wait_ge(hT_a, t + 1)
                pe.wait_ge(hT_v, t + 1)
                for k in range(KC):
                    last = mm(ps[:, LOGITS, t * NE:(t + 1) * NE], tT[:, k, t * P:(t + 1) * P], wr[:, k, :], start=k == 0, stop=k == KC - 1)
                last.then_inc(logits, 1)

            transpose_h(0)
            pe.wait_ge(oT_sb, 3)
            out_project(1, mixA, NG, range(2)).then_inc(half_used, 1)
            pe.wait_ge(wr_ready, 1)
            route(0)
            for c in range(2):
                out_project(1, mixA, NG, range(2, 4), [c]).then_inc(h_psum, 1)

            def open_sums(t, c):
                return mm(ps[:, ACC[t] + c, :], ident, X[:, t, 512 * c:512 * c + 512], start=True, stop=True)

            open_sums(0, 0)
            transpose_h(1)
            open_sums(0, 1).then_inc(opened, 1)
            route(1)
            open_sums(1, 0)
            pe.wait_ge(order_ready, 2)
            pe.wait_ge(picked, T)
            mm(ps[:, RANKS, 0:32], tri[:, :], sel[:, 0, :], start=True, stop=True)
            mm(ps[:, RANKS, 32:64], ones[:, :], sel[:, 0, :], start=True, stop=False)
            mm(ps[:, RANKS, 32:64], tri[:, :], sel[:, 1, :], start=False, stop=True)
            mm(ps[:, RANKS, 64:96], ones[:, :], sel[:, 0, :], start=True, stop=False)
            mm(ps[:, RANKS, 64:96], ones[:, :], sel[:, 1, :], start=False, stop=True).then_inc(ranks, 1)
            open_sums(1, 1).then_inc(opened, 1)

            def gather(n):
                pe.wait_ge(s_ready, n + 1)
                for k in range(KC):
                    for t in range(T):
                        last = mm(ps[:, GAT, k * SLOTS:(k + 1) * SLOTS], N2[:, t, k * P:(k + 1) * P], S1[:, t, :], start=t == 0, stop=t == T - 1)
                last.then_inc(gathered, 1)

            pe.wait_ge(n2_sb, T)
            gather(0)
            pe.wait_ge(gates, T)
            for t in range(T):
                last = nc.tensor.transpose(ps[0:NE, DWN, t * P:(t + 1) * P], Gd[:, t, :], ident)
            last.then_inc(GdT_psum, 1)
            pe.wait_ge(split, 5)
            pe.wait_ge(count_ready, 1)

            def to_tokens():
                return [[mm(ps[:, ACC[t] + j, :], GT[64 * j:64 * j + 64, t, :], ye[64 * j:64 * j + 64, :],
                            start=False, stop=True, skip_group_check=True) for j in range(2)] for t in range(T)]

            def expert(turn, u, step=None, early=None):
                n = turn * TURN + u

                def piece(c, chunks):
                    slot = (u * PIECES + c) % RING
                    return ring[:, slot * PIECE:(slot + 1) * PIECE].rearrange("p (k n) -> p k n", k=chunks)

                def wait_landed(c):
                    s = u * PIECES + c
                    less = 16 if step == "more" and s % RING >= RING - 3 else 0
                    less -= 16 if s % RING == RING - 1 else 0
                    pe.wait_ge(landed[s % RING], turn * (16 * TP // RING) + (16 * (s // RING + 1) - less))

                def gate_up(lhs, halves, start, stop, banks=range(2)):
                    for b in banks:
                        for j in range(2):
                            last = mm(ps[64 * j:64 * j + 64, GU + b, :].rearrange("p (f n) -> p f n", f=2), lhs,
                                      halves[j][:, :, 256 * b:256 * b + 256], start=start, stop=stop)
                    return last

                def halves_of(row):
                    both = row.rearrange("p (f j n) -> p j f n", f=2, j=2)
                    return both[:, 0], both[:, 1]

                pe.wait_ge(xe_sb, n + 1)
                for c in range(GU_PIECES):
                    by_chunk = step == "last" and c == GU_PIECES - 1
                    if not by_chunk and (c > 0 or early is None):
                        wait_landed(c)
                    for k in range(2):
                        if by_chunk:
                            pe.wait_ge(landed_last[k], 16)
                        halves = halves_of(piece(c, 2)[:, k, :])
                        if c + k == 0 and early is not None:
                            pe.wait_ge(ld_ahead[early], 32)
                            halves = ahead[2 * early:2 * early + 2]
                        elif c == 0 and early is not None:
                            wait_landed(0)
                        if 2 * c + k < KC - 1:
                            last = gate_up(xe[:, 2 * c + k, :], halves, c + k == 0, False)
                    if c < GU_PIECES - 1:
                        last.then_inc(pieces_used, 1)
                    if c == 0 and step != "first":
                        pe.wait_ge(gt_sb, n)
                        pe.wait_ge(y_sb, n)
                        to_tokens()
                pe.wait_ge(oneh_ready, n + 1)
                for b in range(2):
                    last = gate_up(xe[:, KC - 1, :], halves, False, False, [b])
                    if b == 1:
                        last.then_inc(pieces_used, 1)
                    gate_up(oneh[:, :], halves_of(bgs[:, :]), False, True, [b]).then_inc(gu_done, 1)

                gather(n + 1)
                for b in range(2):
                    pe.wait_ge(act_ready, n * 2 + b + 1)
                    for c in range(2):
                        last = nc.tensor.transpose(ps[:, DWN, (2 * b + c) * P:(2 * b + c + 1) * P], ab[:, b, c * P:(c + 1) * P], ident)
                    last.then_inc(aT_psum, 1)
                pe.wait_ge(xe_sb, n + 2)
                pe.wait_ge(sg_ready, n + 1)
                for t in range(T):
                    last = nc.tensor.transpose(ps[:, GAT, t * P:(t + 1) * P], SG[:, t, :], ident)
                last.then_inc(gt_psum, 1)

                pe.wait_ge(aT_sb, n + 1)
                for c in range(GU_PIECES, PIECES):
                    first_ahead = early == 0 and c == GU_PIECES
                    if step != "last" and not first_ahead:
                        wait_landed(c)
                    for k in range(4):
                        rows = piece(c, 4)[:, k, :]
                        if first_ahead and k == 0:
                            pe.wait_ge(ld_down_ahead, 16)
                            rows = down_ahead
                        elif first_ahead and k == 1:
                            wait_landed(c)
                        if step == "last":
                            pe.wait_ge(landed_last[2 + 4 * (c - GU_PIECES) + k], 16)
                        for j in range(2):
                            last = mm(ps[64 * j:64 * j + 64, DWN, :], aT[:, k, 64 * (c - GU_PIECES):64 * (c - GU_PIECES) + 64],
                                      rows[:, 512 * j:512 * j + 512],
                                      start=c == GU_PIECES and k == 0, stop=c == PIECES - 1 and k == 3)
                    last.then_inc(pieces_used, 1)

            for u in range(TURN):
                expert(0, u, "first" if u == 0 else None)
            with pe.Fori(1, TURNS - 2) as r:
                for u in range(TURN):
                    expert(r, u)
            for u in range(TURN):
                expert(TURNS - 2, u, early=u)
            pe.wait_ge(ld_bdn, 16)
            pe.wait_ge(GdT_sb, 1)
            for t in range(T):
                for c in range(2):
                    mm(ps[:, ACC[t] + c, :], GdT[:, t, :], bdn[:, 512 * c:512 * c + 512], start=False, stop=True, skip_group_check=True)
            for u in range(TURN):
                expert(TURNS - 1, u, "last" if u == TURN - 1 else None, TURN + u if TURN + u < AHEAD else None)

            def next_pass(p, r):
                for u in range(TURN):
                    expert(p * TURNS + r, u, "more")

            def last_pass_done():
                pe.wait_ge(gt_sb, PASSES * NE)
                pe.wait_ge(y_sb, PASSES * NE)

            more_passes(pe, TURNS, next_pass, last_pass_done)
            pe.wait_ge(gt_sb, NE)
            pe.wait_ge(y_sb, NE)
            for tile in to_tokens():
                for last in tile:
                    last.then_inc(acc_final, 1)


_INS = ["x", "positions", "norm1_w", "w_in", "q_norm_w", "k_norm_w", "sinks", "pool_w", "pool_scale", "w_out",
        "norm2_w", "w_router", "b_router", "w_gu", "b_gu", "w_down", "b_down"]


def kernel(**inputs):
    import concourse.bacc as bacc
    from concourse.bass_utils import run_bass_kernel_spmd

    nc = bacc.Bacc("TRN2", target_bir_lowering=False, num_devices=1)
    arrays = {f"{name}_dram": np.ascontiguousarray(inputs[name]) for name in _INS}
    arrays["consts_dram"], arrays["bands_dram"] = shape_constants()
    args = [nc.dram_tensor(name, a.shape, mybir.dt.from_np(a.dtype), kind="ExternalInput").ap() for name, a in arrays.items()]
    out = nc.dram_tensor("out_dram", arrays["x_dram"].shape, F32, kind="ExternalOutput").ap()
    layer_kernel(nc, *args, out)
    r = run_bass_kernel_spmd(nc, [arrays], core_ids=[0])
    return r.results[0]["out_dram"]
```
